# Optimizing a Trainium2 kernel written in Bass

```python
import math
import jax, jax.numpy as jnp
from jax import lax
import numpy as np

D_MODEL = 1024
BATCH = 1
SEQ = 1024
DEPTH = 1

MIX_WIDTH = D_MODEL
SGU_WIDTH = MIX_WIDTH // 2
SGU_GROUPS = 8
SGU_GROUP_DIM = SGU_WIDTH // SGU_GROUPS
CHUNK = 128
DIFF_WIDTH = MIX_WIDTH - SGU_WIDTH
DIFF_HEADS = 4
DIFF_HEAD_DIM = DIFF_WIDTH // (2 * DIFF_HEADS)
DIFF_V_DIM = 2 * DIFF_HEAD_DIM
Q_BLOCK = 128
REL_BUCKETS = 32
REL_MAX_DIST = 128
PEER_HEADS = 8
PEER_N_KEYS = 128
PEER_EXPERTS = PEER_N_KEYS * PEER_N_KEYS
PEER_TOPK = 16
PEER_KEY_DIM = 256
PEER_HALF = PEER_KEY_DIM // 2
PEER_TOKEN_BLOCK = 128
IN_COLS = 2 * SGU_WIDTH + 3 * DIFF_WIDTH
N_ADA = 6
EPS = 1e-6

kernel_name = "hybrid_sgu_diffattn_peer_block"

def rms_norm(x, g):
    xf = x.astype(jnp.float32)
    y = xf * lax.rsqrt(jnp.mean(xf * xf, axis=-1, keepdims=True) + EPS)
    return (y * g.astype(jnp.float32)).astype(x.dtype)

def layer_norm(x, g, b):
    xf = x.astype(jnp.float32)
    mu = jnp.mean(xf, axis=-1, keepdims=True)
    var = jnp.mean(jnp.square(xf - mu), axis=-1, keepdims=True)
    y = (xf - mu) * lax.rsqrt(var + EPS)
    return (y * g.astype(jnp.float32) + b.astype(jnp.float32)).astype(x.dtype)

def rel_bucket(dist):
    n = jnp.maximum(dist, 0)
    max_exact = REL_BUCKETS // 2
    nf = jnp.maximum(n, 1).astype(jnp.float32)
    large = max_exact + (jnp.log(nf / max_exact) / math.log(REL_MAX_DIST / max_exact)
                         * (REL_BUCKETS - max_exact)).astype(jnp.int32)
    large = jnp.minimum(large, REL_BUCKETS - 1)
    return jnp.where(n < max_exact, n, large)

def spatial_gating(u, v, ln_g, ln_b, w_s, b_s):
    B, S, _ = v.shape
    v = layer_norm(v, ln_g, ln_b)
    nc = S // CHUNK
    vc = v.reshape(B, nc, CHUNK, SGU_GROUPS, SGU_GROUP_DIM)
    w = w_s * jnp.tril(jnp.ones((CHUNK, CHUNK), w_s.dtype))
    mixed = jnp.einsum('gts,bcsgd->bctgd', w, vc) + b_s.T[None, None, :, :, None]
    return u * mixed.reshape(B, S, SGU_WIDTH)

def diff_attention(q, k, v, rel_bias, lam, subln_g, lam_init):
    B, S = q.shape[:2]
    nq = S // Q_BLOCK
    scale = DIFF_HEAD_DIM ** -0.5
    qb = q.reshape(B, nq, Q_BLOCK, DIFF_HEADS, 2, DIFF_HEAD_DIM).transpose(1, 0, 2, 3, 4, 5)
    k_pos = jnp.arange(S)

    def block(args):
        q_blk, i = args
        q_pos = i * Q_BLOCK + jnp.arange(Q_BLOCK)
        dist = q_pos[:, None] - k_pos[None, :]
        bias = rel_bias[rel_bucket(dist)].astype(jnp.float32)
        logits = jnp.einsum('bqhcd,bkhcd->bhcqk', q_blk, k).astype(jnp.float32) * scale
        logits = logits + bias.transpose(2, 0, 1)[None, :, None]
        logits = jnp.where((dist >= 0)[None, None, None], logits, -jnp.inf)
        p = jax.nn.softmax(logits, axis=-1)
        attn = p[:, :, 0] - lam * p[:, :, 1]
        return jnp.einsum('bhqk,bkhe->bqhe', attn.astype(v.dtype), v)

    out = lax.map(block, (qb, jnp.arange(nq)))
    out = out.transpose(1, 0, 2, 3, 4).reshape(B, S, DIFF_HEADS, DIFF_V_DIM)
    out = rms_norm(out, subln_g) * (1.0 - lam_init)
    return out.reshape(B, S, DIFF_HEADS * DIFF_V_DIM)

def peer(h, w_query, sub_keys, expert_u, expert_v):
    B, S, D = h.shape
    T = B * S
    hf = h.reshape(T, D)
    q = (hf @ w_query).reshape(T, PEER_HEADS, 2, PEER_HALF)
    scores = jnp.einsum('thcd,hcnd->thcn', q, sub_keys).astype(jnp.float32)
    s1, i1 = lax.top_k(scores[:, :, 0], PEER_TOPK)
    s2, i2 = lax.top_k(scores[:, :, 1], PEER_TOPK)
    cand_s = (s1[..., :, None] + s2[..., None, :]).reshape(T, PEER_HEADS, PEER_TOPK * PEER_TOPK)
    cand_i = (i1[..., :, None] * PEER_N_KEYS + i2[..., None, :]).reshape(T, PEER_HEADS, PEER_TOPK * PEER_TOPK)
    top_s, pos = lax.top_k(cand_s, PEER_TOPK)
    idx = jnp.take_along_axis(cand_i, pos, axis=-1)
    gates = jax.nn.softmax(top_s, axis=-1).astype(h.dtype)

    nb = T // PEER_TOKEN_BLOCK

    def block(args):
        x_b, idx_b, g_b = args
        u = expert_u[idx_b]
        act = jax.nn.gelu(jnp.einsum('thkd,td->thk', u, x_b))
        vv = expert_v[idx_b]
        return jnp.einsum('thk,thkd->td', g_b * act, vv)

    out = lax.map(block, (hf.reshape(nb, PEER_TOKEN_BLOCK, D),
                          idx.reshape(nb, PEER_TOKEN_BLOCK, PEER_HEADS, PEER_TOPK),
                          gates.reshape(nb, PEER_TOKEN_BLOCK, PEER_HEADS, PEER_TOPK)))
    return out.reshape(B, S, D)

def setup_inputs(seed: int = 0) -> dict:
    key = jax.random.key(seed)
    ks = jax.random.split(key, 20)
    f32 = jnp.float32
    D = D_MODEL
    nrm = lambda k, shape, s: jax.random.normal(k, shape, f32) * s
    return {
        "x": nrm(ks[0], (BATCH, SEQ, D), 1.0),
        "c": nrm(ks[1], (BATCH, D), 1.0),
        "w_ada": nrm(ks[2], (DEPTH, D, N_ADA * D), 0.5 * D ** -0.5),
        "b_ada": nrm(ks[3], (DEPTH, N_ADA * D), 0.01),
        "norm_g": 1.0 + nrm(ks[4], (DEPTH, 4, D), 0.05),
        "w_in": nrm(ks[5], (DEPTH, D, IN_COLS), D ** -0.5),
        "sgu_ln_g": 1.0 + nrm(ks[6], (DEPTH, SGU_WIDTH), 0.05),
        "sgu_ln_b": nrm(ks[7], (DEPTH, SGU_WIDTH), 0.01),
        "sgu_w": nrm(ks[8], (DEPTH, SGU_GROUPS, CHUNK, CHUNK), CHUNK ** -0.5),
        "sgu_b": 1.0 + nrm(ks[9], (DEPTH, SGU_GROUPS, CHUNK), 0.1),
        "diff_lambda": nrm(ks[10], (DEPTH, 4, DIFF_HEAD_DIM), 0.1),
        "diff_subln_g": 1.0 + nrm(ks[11], (DEPTH, DIFF_V_DIM), 0.05),
        "rel_bias": nrm(ks[12], (REL_BUCKETS, DIFF_HEADS), 0.5),
        "w_out": nrm(ks[13], (DEPTH, MIX_WIDTH, D), MIX_WIDTH ** -0.5),
        "peer_w_query": nrm(ks[14], (DEPTH, D, PEER_HEADS * PEER_KEY_DIM), D ** -0.5),
        "peer_sub_keys": nrm(ks[15], (DEPTH, PEER_HEADS, 2, PEER_N_KEYS, PEER_HALF), PEER_HALF ** -0.5),
        "peer_u": nrm(ks[16], (DEPTH, PEER_EXPERTS, D), D ** -0.5),
        "peer_v": nrm(ks[17], (DEPTH, PEER_EXPERTS, D), D ** -0.5),
    }

def reference(x, c, w_ada, b_ada, norm_g, w_in, sgu_ln_g, sgu_ln_b, sgu_w, sgu_b,
              diff_lambda, diff_subln_g, rel_bias, w_out, peer_w_query, peer_sub_keys,
              peer_u, peer_v):
    B, S, D = x.shape
    for l in range(DEPTH):
        mod = (jax.nn.silu(c) @ w_ada[l] + b_ada[l]).reshape(B, N_ADA, D)
        shift1, scale1, gate1, shift2, scale2, gate2 = [mod[:, i, None, :] for i in range(N_ADA)]

        h = rms_norm(x, norm_g[l, 0]) * (1.0 + scale1) + shift1
        z = h @ w_in[l]
        zs = jax.nn.gelu(z[..., :2 * SGU_WIDTH])
        a_out = spatial_gating(zs[..., :SGU_WIDTH], zs[..., SGU_WIDTH:],
                               sgu_ln_g[l], sgu_ln_b[l], sgu_w[l], sgu_b[l])
        zd = z[..., 2 * SGU_WIDTH:]
        q = zd[..., :DIFF_WIDTH].reshape(B, S, DIFF_HEADS, 2, DIFF_HEAD_DIM)
        k = zd[..., DIFF_WIDTH:2 * DIFF_WIDTH].reshape(B, S, DIFF_HEADS, 2, DIFF_HEAD_DIM)
        v = zd[..., 2 * DIFF_WIDTH:].reshape(B, S, DIFF_HEADS, DIFF_V_DIM)
        lam_init = 0.8 - 0.6 * math.exp(-0.3 * l)
        lp = diff_lambda[l].astype(jnp.float32)
        lam = jnp.exp(jnp.sum(lp[0] * lp[1])) - jnp.exp(jnp.sum(lp[2] * lp[3])) + lam_init
        b_out = diff_attention(q, k, v, rel_bias, lam, diff_subln_g[l], lam_init)
        y = jnp.concatenate([a_out, b_out], axis=-1) @ w_out[l]
        x = x + gate1 * rms_norm(y, norm_g[l, 1])

        h = rms_norm(x, norm_g[l, 2]) * (1.0 + scale2) + shift2
        y = peer(h, peer_w_query[l], peer_sub_keys[l], peer_u[l], peer_v[l])
        x = x + gate2 * rms_norm(y, norm_g[l, 3])
    return x


_drawn_inputs = setup_inputs


def setup_inputs(seed=0):
    import zlib

    import numpy as np

    out = dict(_drawn_inputs(seed))
    spreads = {}
    factors = {'sgu_ln_b': 5.417}
    for name, (base, spread) in spreads.items():
        noise = np.random.default_rng([zlib.crc32(name.encode()), seed]).standard_normal(out[name].shape)
        drawn = base * np.exp(spread * noise) if base else spread * noise
        out[name] = __import__('jax').numpy.asarray(drawn.astype(out[name].dtype))
    for name, factor in factors.items():
        out[name] = (out[name] * factor).astype(out[name].dtype)
    return out
```

```python
import math

import concourse.bass as bass
from concourse import mybir
from contextlib import ExitStack
import numpy as np

F32 = mybir.dt.float32
F32R = mybir.dt.float32r
U32 = mybir.dt.uint32
I32 = mybir.dt.int32
ALU = mybir.AluOpType
ACT = mybir.ActivationFunctionType
AX = mybir.AxisListType

P = 128
D = 1024
DC = D // P
S = 1024
TT = S // P
HALF = 512
HEADS = 8
TOPK = 16
NKEY = 128
HC = 2 * HEADS
ETILES = NKEY
NQ = HC
LOWEST = -3.0e38
GT = 8
GBLK = 32
EPS = 1e-6


class Chain:

    def __init__(self, eng, sem):
        self.eng, self.sem, self.n = eng, sem, 0

    def done(self, ins):
        self.n += 1
        return ins.then_inc(self.sem, 1)

    def sync(self, back=0):
        if self.n - back > 0:
            self.eng.wait_ge(self.sem, self.n - back)

    def reset(self):
        self.sync()
        self.eng.sem_clear(self.sem)
        self.n = 0


def loop(nc, eng, start, end):
    return nc.Fori(start, end, engines=[eng.engine], hint_back_edge=True)


def route_and_up(nc, h_hi, h_lo, cols, keys_t, scores, act_d, gate_d):
    with ExitStack() as ctx:
        sb = lambda n, s, d=F32: ctx.enter_context(nc.sbuf_tensor(n, s, d))
        sem = lambda n: ctx.enter_context(nc.semaphore(n))
        raw = sb("col_raw", [P, 2, DC, P])
        c_hi = sb("col_hi", [P, 2, DC, P], F32R)
        c_lo = sb("col_lo", [P, 2, DC, P], F32R)
        res = sb("res", [P, 2, S])
        keys = sb("keys", [P, HC, NKEY])
        sc_out = sb("sc_out", [P, 2, TT, NKEY])
        sc_in = sb("sc_in", [P, 2, 2, NKEY])
        onehot1 = sb("onehot1", [P, 2, GT, NKEY])
        p_hi = sb("p_hi", [P, 2, GT, NKEY], F32R)
        p_lo = sb("p_lo", [P, 2, GT, NKEY], F32R)
        q_oh = sb("q_oh", [P, 2, GT, NKEY], F32R)
        g_buf = sb("g_buf", [P, ETILES, GBLK])
        iota = sb("iota", [P, NKEY])
        iota_i = sb("iota_i", [P, NKEY], I32)
        ident = sb("ident", [P, P])
        work = sb("work", [P, 2, NKEY])
        top = sb("top", [P, 2, TOPK])
        topi = sb("topi", [P, 2, TOPK], U32)
        topf = sb("topf", [P, 2, TOPK])
        cand = sb("cand", [P, TOPK, TOPK])
        cand2 = sb("cand2", [P, TOPK, TOPK])
        best = sb("best", [P, TOPK])
        pos = sb("pos", [P, TOPK], U32)
        pos2 = sb("pos2", [P, 2, TOPK], U32)
        pick = sb("pick", [P, 2, TOPK, TOPK])
        pick2 = sb("pick2", [P, 2, TOPK, TOPK])
        idx = sb("idx", [P, 2, HEADS * TOPK])
        shifted = sb("shifted", [P, HEADS * TOPK])
        expd = sb("expd", [P, HEADS, TOPK])
        esum = sb("esum", [P, HEADS])
        einv = sb("einv", [P, HEADS])
        rt = sb("rt", [P, 3, P])
        idx_t = sb("idx_t", [P, 2, P])
        gate_hi = sb("gate_hi", [P, P], F32R)
        gate_lo = sb("gate_lo", [P, P], F32R)
        ps_up = ctx.enter_context(nc.psum_tensor("ps_up", [P, 2, 2, HALF], F32))
        ps_g = ctx.enter_context(nc.psum_tensor("ps_g", [P, 2, GT, NKEY], F32))

        keys_in = sem("keys_in")
        raw_in = [sem("raw_in0"), sem("raw_in1")]
        hi_done, lo_done, up_done, res_done = sem("hi_done"), sem("lo_done"), sem("up_done"), sem("res_done")
        res_out = [sem("res_out0"), sem("res_out1")]
        sc_mm, sc_copied = sem("sc_mm"), sem("sc_copied")
        sc_stored = [sem("sc_stored0"), sem("sc_stored1")]
        sc_loaded = [sem("sc_loaded0"), sem("sc_loaded1")]
        head_read = sem("head_read")
        tile_routed, exp_done, gates_done = sem("tile_routed"), sem("exp_done"), sem("gates_done")
        turned, turn_copied = sem("turned"), sem("turn_copied")
        eq_ready, q_ready, p_ready = sem("eq_ready"), sem("q_ready"), sem("p_ready")
        g_done, g_copied, g_stored = sem("g_done"), sem("g_copied"), sem("g_stored")
        consts = sem("consts")
        consts2 = sem("consts2")
        dve_step = sem("dve_step")
        last_n = NQ + ETILES - 1

        def isint(x):
            return isinstance(x, int)

        block = ctx.enter_context(nc.Block())

        def supersteps(eng, quarter):
            with loop(nc, eng, 0, TT - 1) as s:
                quarter(s, 0)
                with loop(nc, eng, 1, 4) as v:
                    quarter(s, v)
            quarter(TT - 1, 0)
            with loop(nc, eng, 1, 3) as v:
                quarter(TT - 1, v)
            quarter(TT - 1, 3)

        @block.sync
        def _(sp):
            sp.dma_start(raw[:, 0], cols[0]).then_inc(raw_in[0], 16)
            sp.dma_start(raw[:, 1], cols[1]).then_inc(raw_in[1], 16)
            sp.dma_start(keys[:], keys_t).then_inc(keys_in, 16)
            sp.wait_ge(lo_done, 1)
            sp.dma_start(raw[:, 0], cols[2]).then_inc(raw_in[0], 16)

            def load_ahead(n, b):
                sp.wait_ge(lo_done, n + 2)
                nxt = cols[n + 3] if isint(n) else cols[bass.ds(n + 3, 1)].rearrange("o p c n -> (o p) c n")
                sp.dma_start(raw[:, 1 - b], nxt).then_inc(raw_in[1 - b], 16)

            with loop(nc, sp, 0, HEADS) as u:
                load_ahead(2 * u, 0)
                load_ahead(2 * u + 1, 1)
                for c in range(2):
                    sp.wait_ge(sc_copied, 2 * u + c + 1)
                    dst = scores[:, bass.ds(u, 1), :, c, :].rearrange("a h t n -> t (a h) n")
                    sp.dma_start(dst, sc_out[:, c]).then_inc(sc_stored[c], 16)
            for c in range(2):
                sp.wait_ge(sc_stored[c], 16 * HEADS)

            def quarter(s, v):
                if not (isint(s) and s == TT - 1):
                    for j in range(2):
                        sp.wait_ge(head_read, 8 * s + 2 * v + j + HEADS - 1)
                        src = scores[bass.ds(s + 1, 1), bass.ds(2 * v + j, 1)].rearrange("a h t c n -> (a h t) c n")
                        sp.dma_start(sc_in[:, j], src).then_inc(sc_loaded[j], 16)
                for q in range(4):
                    e = 16 * s + 4 * v + q
                    n = e + NQ
                    if not isint(n) or n + 3 <= last_n:
                        load_ahead(n, q % 2)
                    sp.wait_ge(res_done, n + 1)
                    dst = act_d[bass.ds(e, 1)].rearrange("o p t -> (o p) t")
                    sp.dma_start(dst, res[:, q % 2]).then_inc(res_out[q % 2], 16)
                blk = 4 * s + v
                sp.wait_ge(g_copied, 4 * blk + 4)
                sp.dma_start(gate_d[bass.ds(blk, 1)].rearrange("o p j t -> (o p) j t"), g_buf[:]).then_inc(g_stored, 16)

            supersteps(sp, quarter)
            sp.wait_ge(g_stored, 16 * (S // GBLK))
            for b in range(2):
                sp.wait_ge(res_out[b], 16 * ETILES // 2)

        @block.scalar
        def _(act):
            def split_hi(n, b):
                half = n // 2 if isint(n) else None
                return half

            def hi(n, k, b):
                act.wait_ge(raw_in[b], 16 * k)
                if not isint(n) or n >= 2:
                    act.wait_ge(up_done, n - 1)
                nc.scalar.activation(c_hi[:, b], raw[:, b], ACT.Copy).then_inc(hi_done, 1)

            hi(0, 1, 0)
            with loop(nc, act, 0, HEADS) as u:
                for b in range(2):
                    n = 2 * u + b
                    act.wait_ge(raw_in[1 - b], 16 * (u + 1 + b))
                    act.wait_ge(up_done, n)
                    nc.scalar.activation(c_hi[:, 1 - b], raw[:, 1 - b], ACT.Copy).then_inc(hi_done, 1)
                    act.wait_ge(up_done, n + 1)
                    act.wait_ge(sc_mm, 2 * u)
                    nc.scalar.activation(res[:, b], ps_up[:, b], ACT.Copy).then_inc(res_done, 1)
                for c in range(2):
                    act.wait_ge(sc_mm, 2 * u + c + 1)
                    act.wait_ge(sc_stored[c], 16 * u)
                    act.wait_ge(head_read, u)
                    nc.scalar.activation(sc_out[:, c], ps_g[:, c], ACT.Copy).then_inc(sc_copied, 1)

            def copy_gates(s, v, q):
                g = 16 * s + 4 * v + q
                if q == 0:
                    act.wait_ge(g_stored, 16 * (4 * s + v))
                act.wait_ge(g_done, g + 1)
                nc.scalar.activation(g_buf[:, :, GT * q:GT * q + GT], ps_g[:, q % 2].rearrange("p t j -> p j t"),
                                     ACT.Copy).then_inc(g_copied, 1)

            def quarter(s, v):
                for q in range(4):
                    b = q % 2
                    e = 16 * s + 4 * v + q
                    n = e + NQ
                    k = 8 * s + 2 * v + q // 2
                    if not isint(n) or n + 1 <= last_n:
                        act.wait_ge(raw_in[1 - b], 16 * (k + NQ // 2 + 1 + b))
                        act.wait_ge(up_done, n)
                        nc.scalar.activation(c_hi[:, 1 - b], raw[:, 1 - b], ACT.Copy).then_inc(hi_done, 1)
                    if isint(v) and v == 0 and q == 0:
                        act.wait_ge(tile_routed, s + 1)
                        nc.scalar.activation(expd[:].rearrange("p h k -> p (h k)"), shifted[:], ACT.Exp).then_inc(exp_done, 1)
                    act.wait_ge(up_done, n + 1)
                    act.wait_ge(res_out[b], 16 * k)
                    nc.scalar.activation(res[:, b], ps_up[:, b], ACT.Gelu_apprx_tanh).then_inc(res_done, 1)
                    if not (isint(v) and v == 0):
                        copy_gates(s, v, q)
                    elif q > 0:
                        copy_gates(s, v, q - 1)
                        if q == 3:
                            copy_gates(s, v, 3)

            supersteps(act, quarter)

        @block.tensor
        def _(pe):
            def up(n, b):
                pe.wait_ge(hi_done, n + 1)
                pe.wait_ge(lo_done, n + 1)
                if not isint(n) or n >= 2:
                    pe.wait_ge(res_done, n - 1)
                for k in range(DC):
                    for i, (w, h) in enumerate(((c_hi, h_hi), (c_hi, h_lo), (c_lo, h_hi))):
                        for half in range(2):
                            mm = pe.matmul(ps_up[:, b, half], w[:, b, k], h[:, k, half * HALF:half * HALF + HALF],
                                           start=(k == 0 and i == 0), stop=(k == DC - 1 and i == 2))
                mm.then_inc(up_done, 1)

            def head(u, first):
                for b in range(2):
                    n = 2 * u + b
                    up(n, b)
                pe.wait_ge(keys_in, 16)
                for c in range(2):
                    pe.wait_ge(res_done, 2 * u + c + 1)
                    pe.wait_ge(sc_copied, 2 * u)
                    for t in range(TT):
                        mm = pe.matmul(ps_g[:, c, t], res[:, c, t * P:t * P + P], key_at(u, c), start=True, stop=True)
                    mm.then_inc(sc_mm, 1)

            def key_at(u, c):
                if isint(u):
                    return keys[:, 2 * u + c]
                return keys[:, bass.ds(2 * u + c, 1)].rearrange("p o n -> p (o n)")

            head(0, True)
            with loop(nc, pe, 1, HEADS) as u:
                head(u, False)
            pe.wait_ge(sc_copied, 2 * HEADS)

            def turn(s):
                pe.wait_ge(consts, 4)
                pe.wait_ge(gates_done, s + 1)
                pe.wait_ge(g_copied, 16 * s)
                for i in range(3):
                    mm = pe.transpose(ps_g[:, 0, i], rt[:, i], ident[:])
                mm.then_inc(turned, 1)

            def gates(s, v, q):
                g = 16 * s + 4 * v + q
                pe.wait_ge(p_ready, 2 * g + 2)
                pe.wait_ge(q_ready, g + 1)
                if not (isint(v) and v == 0 and q < 2):
                    pe.wait_ge(g_copied, g - 1)
                for t in range(GT):
                    pe.matmul(ps_g[:, q % 2, t], p_hi[:, q % 2, t], q_oh[:, q % 2, t], start=True, stop=False)
                    mm = pe.matmul(ps_g[:, q % 2, t], p_lo[:, q % 2, t], q_oh[:, q % 2, t], start=False, stop=True)
                mm.then_inc(g_done, 1)

            def quarter(s, v):
                first = isint(v) and v == 0
                for q in range(4):
                    up(16 * s + 4 * v + q + NQ, q % 2)
                    if not first:
                        gates(s, v, q)
                    elif q == 0:
                        turn(s)
                    else:
                        gates(s, v, q - 1)
                        if q == 3:
                            gates(s, v, 3)

            supersteps(pe, quarter)

        @block.gpsimd
        def _(pool):
            nc.gpsimd.iota(iota_i[:], [[1, NKEY]], base=0, channel_multiplier=0).then_inc(consts, 1)
            pool.wait_ge(consts, 1)
            nc.gpsimd.tensor_copy(iota[:], iota_i[:]).then_inc(consts, 1)
            nc.gpsimd.memset(ident[:], 0.0).then_inc(consts, 1)
            pool.wait_ge(consts, 3)
            nc.gpsimd.affine_select(out=ident[:], in_=ident[:], compare_op=ALU.not_equal, fill=1.0, base=0,
                                    pattern=[[-1, P]], channel_multiplier=1).then_inc(consts, 1)

            def quarter(s, v):
                for q in range(4):
                    g = 16 * s + 4 * v + q
                    pool.wait_ge(eq_ready, g + 1)
                    for part, out in ((gate_hi, p_hi), (gate_lo, p_lo)):
                        t0 = GT * 4 * v + GT * q
                        col = part[:, bass.ds(t0, GT)].bitcast(F32).unsqueeze(2).to_broadcast([P, GT, NKEY])
                        nc.gpsimd.tensor_tensor(out[:, q % 2], onehot1[:, q % 2], col, ALU.mult).then_inc(p_ready, 1)

            supersteps(pool, quarter)

        @block.vector
        def _(dve):
            ch = Chain(dve, dve_step)

            def lo(n, b):
                dve.wait_ge(hi_done, n + 1)
                nc.vector.tensor_tensor(c_lo[:, b], raw[:, b], c_hi[:, b].bitcast(F32), ALU.subtract).then_inc(lo_done, 1)

            def route(sc, col):
                ch.sync()
                for r in range(2):
                    lo8 = slice(8 * r, 8 * r + 8)
                    src = [sc[c] if r == 0 else work[:, c] for c in range(2)]
                    for c in range(2):
                        if r == 1:
                            ch.sync(1)
                        ch.done(nc.vector.max(top[:, c, lo8], src[c]))
                    for c in range(2):
                        ch.sync(1)
                        ch.done(nc.vector.max_index(topi[:, c, lo8], top[:, c, lo8], src[c]))
                    if r == 0:
                        for c in range(2):
                            ch.done(nc.vector.match_replace(work[:, c], top[:, c, lo8], src[c], LOWEST))
                ch.sync()
                yield
                ch.done(nc.vector.tensor_copy(topf[:], topi[:]))
                ch.done(nc.vector.tensor_tensor(cand[:], top[:, 0].unsqueeze(2).to_broadcast([P, TOPK, TOPK]),
                                                top[:, 1].unsqueeze(1).to_broadcast([P, TOPK, TOPK]), ALU.add))
                flat = cand[:].rearrange("p a b -> p (a b)")
                flat2 = cand2[:].rearrange("p a b -> p (a b)")
                ch.sync()
                ch.done(nc.vector.max(best[:, 0:8], flat))
                ch.sync()
                ch.done(nc.vector.max_index(pos[:, 0:8], best[:, 0:8], flat))
                ch.done(nc.vector.match_replace(flat2, best[:, 0:8], flat, LOWEST))
                ch.sync()
                ch.done(nc.vector.max(best[:, 8:16], flat2))
                ch.sync()
                ch.done(nc.vector.max_index(pos[:, 8:16], best[:, 8:16], flat2))
                ch.done(nc.vector.tensor_scalar(shifted[:, bass.ds(col, TOPK)], best[:], best[:, 0:1], None, ALU.subtract))
                ch.sync()
                ch.done(nc.vector.tensor_scalar(pos2[:, 0], pos[:], 4, None, ALU.logical_shift_right))
                ch.done(nc.vector.tensor_scalar(pos2[:, 1], pos[:], 15, None, ALU.bitwise_and))
                ch.sync()
                ch.done(nc.vector.tensor_tensor(
                    pick[:], pos2[:].unsqueeze(3).to_broadcast([P, 2, TOPK, TOPK]),
                    iota[:, 0:TOPK].unsqueeze(1).unsqueeze(1).to_broadcast([P, 2, TOPK, TOPK]), ALU.is_equal))
                ch.sync()
                ch.done(nc.vector.tensor_tensor(pick2[:], pick[:],
                                                topf[:].unsqueeze(2).to_broadcast([P, 2, TOPK, TOPK]), ALU.mult))
                ch.sync()
                ch.done(nc.vector.tensor_reduce(idx[:, :, bass.ds(col, TOPK)], pick2[:], AX.X, ALU.add))
                ch.sync()

            dve.wait_ge(consts, 4)
            lo(0, 0)
            with loop(nc, dve, 0, HEADS) as u:
                lo(2 * u + 1, 1)
                lo(2 * u + 2, 0)
                dve.wait_ge(sc_copied, 2 * u + 2)
                dve.nop(nofuse=True)
                for _ in route([sc_out[:, c, 0] for c in range(2)], u * TOPK):
                    dve.sem_inc(head_read, 1)
                ch.reset()
            dve.sem_inc(tile_routed, 1)

            def finish_gates(s):
                dve.wait_ge(exp_done, s + 1)
                ch.done(nc.vector.tensor_reduce(esum[:], expd[:], AX.X, ALU.add))
                ch.sync()
                ch.done(nc.vector.reciprocal(einv[:], esum[:]))
                dve.wait_ge(turned, s)
                ch.done(nc.vector.tensor_copy(rt[:, 0:2], idx[:]))
                ch.sync()
                ch.done(nc.vector.tensor_tensor(rt[:, 2].rearrange("p (h k) -> p h k", h=HEADS), expd[:],
                                                einv[:].unsqueeze(2).to_broadcast([P, HEADS, TOPK]), ALU.mult))
                ch.sync()
                dve.sem_inc(gates_done, 1)

            def copy_turned(s):
                dve.wait_ge(turned, s + 1)
                dve.wait_ge(p_ready, 32 * s)
                ch.done(nc.vector.tensor_copy(idx_t[:], ps_g[:, 0, 0:2]))
                ch.done(nc.vector.tensor_copy(gate_hi[:], ps_g[:, 0, 2]))
                ch.sync()
                ch.done(nc.vector.tensor_tensor(gate_lo[:], ps_g[:, 0, 2], gate_hi[:].bitcast(F32), ALU.subtract))
                ch.sync()
                dve.sem_inc(turn_copied, 1)

            def onehots(s, v, q):
                g = 16 * s + 4 * v + q
                b = q % 2
                if not (isint(v) and v == 0 and q < 2):
                    dve.wait_ge(g_done, g - 1)
                    dve.wait_ge(p_ready, 2 * g - 2)
                else:
                    dve.wait_ge(g_done, 16 * s)
                t0 = GT * 4 * v + GT * q
                keyrow = iota[:].unsqueeze(1).to_broadcast([P, GT, NKEY])
                for i, out in ((0, onehot1), (1, q_oh)):
                    col = idx_t[:, i, bass.ds(t0, GT)].unsqueeze(2).to_broadcast([P, GT, NKEY])
                    nc.vector.tensor_tensor(out[:, b], keyrow, col, ALU.is_equal).then_inc((eq_ready, q_ready)[i], 1)

            def quarter(s, v):
                first = isint(v) and v == 0
                tail = isint(s) and s == TT - 1
                for q in range(4):
                    n = 16 * s + 4 * v + q + NQ
                    if not isint(n) or n + 1 <= last_n:
                        lo(n + 1, 1 - q % 2)
                    if first and q == 0:
                        finish_gates(s)
                    if not first:
                        onehots(s, v, q)
                    if q % 2 == 0 and not tail:
                        dve.wait_ge(sc_loaded[q // 2], 16 * (4 * s + v + 1))
                        dve.nop(nofuse=True)
                        for _ in route([sc_in[:, q // 2, c] for c in range(2)], (2 * v + q // 2) * TOPK):
                            dve.sem_inc(head_read, 1)
                    if first:
                        if q == 0:
                            copy_turned(s)
                        onehots(s, v, q)
                if not tail and isint(v) is False:
                    pass
                ch.reset()

            with loop(nc, dve, 0, TT - 1) as s:
                quarter(s, 0)
                with loop(nc, dve, 1, 4) as v:
                    quarter(s, v)
                dve.sem_inc(tile_routed, 1)
            quarter(TT - 1, 0)
            with loop(nc, dve, 1, 3) as v:
                quarter(TT - 1, v)
            quarter(TT - 1, 3)


GROUP = 4
NGROUP = ETILES // GROUP


def down_and_finish(nc, act_d, gate_d, v_cols, x_mid, gain, out):
    with ExitStack() as ctx:
        sb = lambda n, s, d=F32: ctx.enter_context(nc.sbuf_tensor(n, s, d))
        sem = lambda n: ctx.enter_context(nc.semaphore(n))
        v_raw = sb("v_raw", [P, 2, D])
        a_raw = sb("a_raw", [P, 2, S])
        g_raw = sb("g_raw", [P, S // GBLK, GROUP, GBLK])
        v_hi = sb("v_hi", [P, 2, GROUP, D], F32R)
        v_lo = sb("v_lo", [P, 2, GROUP, D], F32R)
        c_hi = sb("coef_hi", [P, 2, GROUP, S], F32R)
        c_lo = sb("coef_lo", [P, 2, GROUP, S], F32R)
        acc = sb("acc", [P, TT, D])
        ss = sb("y_ss", [P, TT])
        rs = sb("y_rs", [P, TT])
        rr = sb("y_rr", [P, TT])
        eps = sb("y_eps", [P, 1])
        ps = ctx.enter_context(nc.psum_tensor("ps_y", [P, 4, 2, HALF], F32))

        v_in = [sem("v_in0"), sem("v_in1")]
        a_in = [sem("a_in0"), sem("a_in1")]
        g_in = sem("g_in")
        coef, coef_hi, coef_lo = sem("coef"), sem("coef_hi_done"), sem("coef_lo_done")
        vhi_done, vlo_done = sem("vhi_done"), sem("vlo_done")
        y_mm, y_added = sem("y_mm"), sem("y_added")
        acc_zero = sem("acc_zero")
        x_in = [sem("x_in0"), sem("x_in1")]
        sq_done, root_done, inv_done, out_ready = sem("sq_done"), sem("root_done"), sem("inv_done"), sem("out_ready")
        stored = sem("stored")
        dve_step = sem("dve_step_b")
        block = ctx.enter_context(nc.Block())

        @block.sync
        def _(sp):
            def gates_in(m):
                if not isinstance(m, int) or m > 0:
                    sp.wait_ge(coef, GROUP * m)
                src = gate_d[:, :, bass.ds(GROUP * m, GROUP), :].rearrange("b p j t -> p b (j t)")
                sp.dma_start(g_raw[:].rearrange("p b j t -> p b (j t)"), src).then_inc(g_in, 16)

            def load(m, j):
                e = GROUP * m + j
                b = j % 2
                if not (isinstance(m, int) and m == 0 and j < 2):
                    sp.wait_ge(coef_lo, e - 1)
                sp.dma_start(a_raw[:, b], act_d[bass.ds(e, 1)].rearrange("o p t -> (o p) t")).then_inc(a_in[b], 16)
                if not (isinstance(m, int) and m == 0 and j < 2):
                    sp.wait_ge(vlo_done, e - 1)
                sp.dma_start(v_raw[:, b], v_cols[bass.ds(e, 1)].rearrange("o p d -> (o p) d")).then_inc(v_in[b], 16)

            gates_in(0)
            for j in range(GROUP):
                load(0, j)
            with loop(nc, sp, 1, NGROUP) as m:
                gates_in(m)
                for j in range(GROUP):
                    load(m, j)
            sp.wait_ge(y_mm, TT * (NGROUP - 1))
            for t in range(TT):
                if t >= 2:
                    sp.wait_ge(out_ready, t - 1)
                else:
                    sp.wait_ge(coef_lo, ETILES)
                sp.dma_start(a_raw[:, t % 2], x_mid[t * P:t * P + P]).then_inc(x_in[t % 2], 16)
                if t >= 1:
                    sp.wait_ge(out_ready, t)
                    sp.dma_start(out[(t - 1) * P:t * P], acc[:, t - 1]).then_inc(stored, 16)
            sp.wait_ge(out_ready, TT)
            sp.dma_start(out[(TT - 1) * P:TT * P], acc[:, TT - 1]).then_inc(stored, 16)
            sp.wait_ge(stored, 16 * TT)

        @block.scalar
        def _(act):
            def split(m, p, j):
                b = j % 2
                act.wait_ge(v_in[b], 16 * (2 * m + j // 2 + 1))
                if not (isinstance(m, int) and m < 2):
                    act.wait_ge(y_mm, TT * (m - 1))
                nc.scalar.activation(v_hi[:, p, j], v_raw[:, b], ACT.Copy).then_inc(vhi_done, 1)
                act.wait_ge(coef, GROUP * m + j + 1)
                nc.scalar.activation(c_hi[:, p, j], a_raw[:, b], ACT.Copy).then_inc(coef_hi, 1)

            for m in range(2):
                for j in range(GROUP):
                    split(m, m, j)
            with loop(nc, act, 1, NGROUP // 2) as w:
                for p in range(2):
                    for j in range(GROUP):
                        split(2 * w + p, p, j)
            for t in range(TT):
                act.wait_ge(y_added, TT * (NGROUP - 1) + t + 1)
                if t >= 2:
                    act.wait_ge(sq_done, t - 1)
                nc.scalar.activation(v_raw[:, t % 2], acc[:, t], ACT.Square, accum_out=ss[:, t:t + 1]).then_inc(sq_done, 1)
                act.wait_ge(sq_done, t + 1)
                nc.scalar.activation(rs[:, t:t + 1], ss[:, t:t + 1], ACT.Sqrt, bias=eps[:], scale=1.0 / D).then_inc(root_done, 1)

        @block.tensor
        def _(pe):
            def group(m, p):
                for t in range(TT):
                    pe.wait_ge(coef_lo, GROUP * m + GROUP)
                    pe.wait_ge(vlo_done, GROUP * m + GROUP)
                    if not (isinstance(m, int) and m == 0 and t < 4):
                        pe.wait_ge(y_added, TT * m + t - 3)
                    for j in range(GROUP):
                        for i, (c, v) in enumerate(((c_hi, v_hi), (c_hi, v_lo), (c_lo, v_hi))):
                            for half in range(2):
                                mm = pe.matmul(ps[:, t % 4, half], c[:, p, j, t * P:t * P + P],
                                               v[:, p, j, half * HALF:half * HALF + HALF],
                                               start=(j == 0 and i == 0), stop=(j == GROUP - 1 and i == 2))
                    mm.then_inc(y_mm, 1)

            group(0, 0)
            group(1, 1)
            with loop(nc, pe, 1, NGROUP // 2) as w:
                group(2 * w, 0)
                group(2 * w + 1, 1)

        @block.vector
        def _(dve):
            nc.vector.memset(acc[:], 0.0).then_inc(acc_zero, 1)
            nc.vector.memset(eps[:], EPS).then_inc(acc_zero, 1)

            def product(m, p, j):
                b = j % 2
                e = GROUP * m + j
                if j == 0:
                    dve.wait_ge(g_in, 16 * (m + 1))
                dve.wait_ge(a_in[b], 16 * (2 * m + j // 2 + 1))
                a = a_raw[:, b].rearrange("p (k t) -> p k t", t=GBLK)
                nc.vector.tensor_tensor(a, a, g_raw[:, :, j], ALU.mult).then_inc(coef, 1)
                dve.wait_ge(vhi_done, e + 1)
                nc.vector.tensor_tensor(v_lo[:, p, j], v_raw[:, b], v_hi[:, p, j].bitcast(F32), ALU.subtract).then_inc(vlo_done, 1)
                dve.wait_ge(coef_hi, e + 1)
                nc.vector.tensor_tensor(c_lo[:, p, j], a_raw[:, b], c_hi[:, p, j].bitcast(F32), ALU.subtract).then_inc(coef_lo, 1)

            def add(m, t):
                if isinstance(m, int) and m == 0:
                    dve.wait_ge(acc_zero, 2)
                else:
                    dve.wait_ge(y_added, TT * m - TT + t + 1)
                dve.wait_ge(y_mm, TT * m + t + 1)
                nc.vector.tensor_tensor(acc[:, t], ps[:, t % 4].rearrange("p a b -> p (a b)"), acc[:, t], ALU.add).then_inc(y_added, 1)

            def step(m, p):
                for j in range(GROUP):
                    product(m + 1, 1 - p, j)
                    add(m, 2 * j)
                    add(m, 2 * j + 1)

            for j in range(GROUP):
                product(0, 0, j)
            step(0, 0)
            with loop(nc, dve, 0, NGROUP // 2 - 1) as w:
                step(2 * w + 1, 1)
                step(2 * w + 2, 0)
            for t in range(TT):
                add(NGROUP - 1, t)
                dve.wait_ge(root_done, t + 1)
                nc.vector.reciprocal(rr[:, t:t + 1], rs[:, t:t + 1]).then_inc(inv_done, 1)
                dve.wait_ge(inv_done, t + 1)
                nc.vector.scalar_tensor_tensor(out=acc[:, t], in0=acc[:, t], scalar=rr[:, t:t + 1], in1=gain[:],
                                               op0=ALU.mult, op1=ALU.mult).then_inc(dve_step, 1)
                dve.wait_ge(dve_step, t + 1)
                dve.wait_ge(x_in[t % 2], 16 * (t // 2 + 1))
                nc.vector.tensor_tensor(acc[:, t], acc[:, t], a_raw[:, t % 2], ALU.add).then_inc(out_ready, 1)



NGRP = 2
COLW = 256
HEADS_A = 4
DH = 64
VD = 128
NADA = 6
LAM_INIT = 0.8 - 0.6 * math.exp(-0.3 * 0)
RB = 32
RLEN = 3 * P - 1
SGU_G = 8
SW = 512


def modulate_and_norm(nc, x, c_col, w_ada, b_ada, norm_g, g_col, ident, h_hi, h_lo, mod_cols, gain1, gain2):
    with ExitStack() as ctx:
        sb = lambda n, s, d=F32: ctx.enter_context(nc.sbuf_tensor(n, s, d))
        sem = lambda n: ctx.enter_context(nc.semaphore(n))
        NW = 4
        wbuf = sb("w_ada_rows", [P, NW, D])
        part = sb("part", [P, 2, D])
        modb = sb("modb", [P, NADA, D])
        bias = sb("bias_rows", [P, D])
        grow = sb("g_rows", [P, 2, D])
        gcol = sb("g_col_s", [P, 4, DC])
        craw = sb("c_raw", [P, DC])
        cs = sb("c_silu", [P, DC])
        ones = sb("ones_f1", [P, P])
        xs = sb("x_tiles", [P, TT, D])
        xr = sb("x_scaled", [P, 2, D])
        hf = sb("h_full", [P, 2, DC, P])
        ssq = sb("ssq", [P, TT])
        rt_ = sb("rt_", [P, TT])
        inv = sb("inv", [P, TT])
        eps = sb("eps_f1", [P, 1])
        ps_m = ctx.enter_context(nc.psum_tensor("ps_m", [P, 2, HALF], F32))
        ps_c = ctx.enter_context(nc.psum_tensor("ps_c", [P, DC, P], F32))
        ps_x = ctx.enter_context(nc.psum_tensor("ps_x", [P, 2, DC, P], F32))
        c_in, small_in, b_in, g_in = sem("c_in"), sem("small_in"), sem("b_in"), sem("grow_in")
        w_in = [sem(f"w_in{i}") for i in range(NW)]
        x_in = [sem(f"xt_in{i}") for i in range(TT)]
        consts, silu_done, part_done, mod_mm, mod_done = sem("consts_f1"), sem("silu_done"), sem("part_done"), sem("mod_mm"), sem("mod_done")
        sliced = sem("sliced")
        sq_done, rt_done, inv_done, xr_done, xt_done, hf_done, hi_done, lo_done = (sem(f"f1_{i}") for i in "sq rt inv xr xt hf hi lo".split())
        cols_mm, cols_done = sem("cols_mm"), sem("cols_done")
        block = ctx.enter_context(nc.Block())

        @block.sync
        def _(sp):
            sp.dma_start(craw[:], c_col).then_inc(c_in, 16)
            for k in range(NW):
                sp.dma_start(wbuf[:, k], w_ada[0, k]).then_inc(w_in[k], 16)
            sp.dma_start(bias[:], b_ada[0:1, 0:D].to_broadcast([P, D])).then_inc(b_in, 16)
            sp.dma_start(gcol[:], g_col).then_inc(small_in, 16)
            for i in range(2):
                sp.dma_start(grow[:, i], norm_g[2 * i + 1:2 * i + 2, :].to_broadcast([P, D])).then_inc([g_in, small_in][i], 16)

            for k in range(NW):
                sp.wait_ge(sliced, k + 1)
                sp.dma_start(wbuf[:, k], w_ada[0, NW + k]).then_inc(w_in[k], 16)
            with loop(nc, sp, 1, NADA) as i:
                for k in range(DC):
                    sp.wait_ge(sliced, 8 * i - 4 + k + 1)
                    sp.dma_start(wbuf[:, k % NW], w_ada[bass.ds(i, 1), k].rearrange("o p n -> (o p) n")).then_inc(w_in[k % NW], 16)
                    if k == 4:
                        sp.wait_ge(mod_done, i)
                        sp.dma_start(bias[:], b_ada[0:1, bass.ds(i * D, D)].to_broadcast([P, D])).then_inc(b_in, 16)

        @block.scalar
        def _(act):
            for t in range(TT):
                act.dma_start(xs[:, t], x[t * P:t * P + P]).then_inc(x_in[t], 16)
            act.wait_ge(c_in, 16)
            nc.scalar.activation(cs[:], craw[:], ACT.Silu).then_inc(silu_done, 1)
            for t in range(TT):
                act.wait_ge(x_in[t], 16)
                if t >= 2:
                    act.wait_ge(sq_done, t - 1)
                nc.scalar.activation(xr[:, t % 2], xs[:, t], ACT.Square, accum_out=ssq[:, t:t + 1]).then_inc(sq_done, 1)
            act.wait_ge(sq_done, TT)
            act.wait_ge(consts, 2)
            nc.scalar.activation(rt_[:], ssq[:], ACT.Sqrt, bias=eps[:], scale=1.0 / D).then_inc(rt_done, 1)
            for t in range(TT):
                act.wait_ge(hf_done, 2 * t + 2)
                nc.scalar.activation(h_hi[:, :, t * P:t * P + P], hf[:, t % 2], ACT.Copy).then_inc(hi_done, 1)

        @block.gpsimd
        def _(pool):
            nc.gpsimd.memset(ident[:], 0.0).then_inc(cols_done, 1)
            pool.wait_ge(cols_done, 1)
            nc.gpsimd.affine_select(out=ident[:], in_=ident[:], compare_op=ALU.not_equal, fill=1.0, base=0,
                                    pattern=[[-1, P]], channel_multiplier=1).then_inc(cols_done, 1)

        @block.tensor
        def _(pe):
            pe.wait_ge(consts, 1)

            def total(i):
                pe.wait_ge(part_done, i + 1)
                if not isinstance(i, int) or i > 0:
                    pe.wait_ge(mod_done, i)
                for half in range(2):
                    mm = pe.matmul(ps_m[:, half], ones[:], part[:, 0, half * HALF:half * HALF + HALF], start=True, stop=True)
                mm.then_inc(mod_mm, 1)

            total(0)
            with loop(nc, pe, 1, NADA) as i:
                total(i)
            pe.wait_ge(cols_done, 2)
            pe.wait_ge(mod_done, NADA)
            for n, i in enumerate((0, 1, 3, 4)):
                if n:
                    pe.wait_ge(cols_done, 2 + n)
                for k in range(DC):
                    mm = pe.transpose(ps_c[:, k], modb[:, i, k * P:k * P + P], ident[:])
                mm.then_inc(cols_mm, 1)
            for t in range(TT):
                pe.wait_ge(xr_done, t + 1)
                if t >= 2:
                    pe.wait_ge(hf_done, 2 * (t - 2) + 1)
                for k in range(DC):
                    mm = pe.transpose(ps_x[:, t % 2, k], xr[:, t % 2, k * P:k * P + P], ident[:])
                mm.then_inc(xt_done, 1)

        @block.vector
        def _(dve):
            nc.vector.memset(ones[:], 1.0).then_inc(consts, 1)
            nc.vector.memset(eps[:], EPS).then_inc(consts, 1)
            dve.wait_ge(silu_done, 1)

            def row(i):
                for k in range(DC):
                    dve.wait_ge(w_in[k % NW], 16 * (2 * i + k // NW + 1))
                    if k == 0:
                        if not isinstance(i, int) or i > 0:
                            dve.wait_ge(mod_mm, i)
                            dve.wait_ge(sliced, 8 * i)
                        nc.vector.tensor_scalar(part[:, 1], wbuf[:, 0], cs[:, 0:1], None, ALU.mult).then_inc(sliced, 1)
                    else:
                        dve.wait_ge(sliced, 8 * i + k)
                        dst, src = (part[:, 0], part[:, 1]) if k % 2 else (part[:, 1], part[:, 0])
                        nc.vector.scalar_tensor_tensor(out=dst, in0=wbuf[:, k % NW], scalar=cs[:, k:k + 1], in1=src,
                                                       op0=ALU.mult, op1=ALU.add).then_inc(sliced, 1)
                dve.wait_ge(sliced, 8 * i + DC)
                dve.sem_inc(part_done, 1)
                dve.wait_ge(mod_mm, i + 1)
                dve.wait_ge(b_in, 16 * (i + 1))
                nc.vector.tensor_tensor(modb[:, i] if isinstance(i, int) else modb[:, bass.ds(i, 1)].rearrange("p o n -> p (o n)"),
                                        ps_m[:].rearrange("p a b -> p (a b)"), bias[:], ALU.add).then_inc(mod_done, 1)

            row(0)
            with loop(nc, dve, 1, NADA) as i:
                row(i)
            dve.wait_ge(mod_done, NADA)
            dve.wait_ge(small_in, 32)
            dve.wait_ge(g_in, 16)
            nc.vector.tensor_tensor(gain1[:], modb[:, 2], grow[:, 0], ALU.mult)
            nc.vector.tensor_tensor(gain2[:], modb[:, 5], grow[:, 1], ALU.mult)
            for n, (i, o) in enumerate(((0, 1), (1, 0), (3, 3), (4, 2))):
                dve.wait_ge(cols_mm, n + 1)
                if i in (0, 3):
                    nc.vector.tensor_copy(mod_cols[:, o], ps_c[:, :, 0]).then_inc(cols_done, 1)
                else:
                    nc.vector.scalar_tensor_tensor(out=mod_cols[:, o], in0=ps_c[:, :, 0], scalar=1.0, in1=gcol[:, 0 if i == 1 else 2],
                                                   op0=ALU.add, op1=ALU.mult).then_inc(cols_done, 1)
            dve.wait_ge(rt_done, 1)
            nc.vector.reciprocal(inv[:], rt_[:]).then_inc(inv_done, 1)
            dve.wait_ge(inv_done, 1)
            dve.wait_ge(cols_done, 6)

            def scaled(t):
                if t >= 2:
                    dve.wait_ge(xt_done, t - 1)
                nc.vector.tensor_scalar(xr[:, t % 2], xs[:, t], inv[:, t:t + 1], None, ALU.mult).then_inc(xr_done, 1)

            scaled(0)
            for t in range(TT):
                if t + 1 < TT:
                    scaled(t + 1)
                dve.wait_ge(xt_done, t + 1)
                if t >= 2:
                    dve.wait_ge(lo_done, t - 1)
                    dve.wait_ge(hi_done, t - 1)
                affine_cols(nc, dve, hf[:, t % 2], ps_x[:, t % 2], mod_cols[:, 0], mod_cols[:, 1], hf_done, 2 * t)
                dve.wait_ge(hf_done, 2 * t + 2)
                dve.wait_ge(hi_done, t + 1)
                nc.vector.tensor_tensor(h_lo[:, :, t * P:t * P + P], hf[:, t % 2], h_hi[:, :, t * P:t * P + P].bitcast(F32),
                                        ALU.subtract).then_inc(lo_done, 1)


def affine_cols(nc, dve, out, src, scale, shift, step, before):
    nc.vector.tensor_tensor(out, src, scale.unsqueeze(2).to_broadcast([P, DC, P]), ALU.mult).then_inc(step, 1)
    dve.wait_ge(step, before + 1)
    nc.vector.tensor_tensor(out, out, shift.unsqueeze(2).to_broadcast([P, DC, P]), ALU.add).then_inc(step, 1)


def in_project(nc, w_in, h_hi, h_lo, z_t, z_n):
    with ExitStack() as ctx:
        sb = lambda n, s, d=F32: ctx.enter_context(nc.sbuf_tensor(n, s, d))
        sem = lambda n: ctx.enter_context(nc.semaphore(n))
        raw = sb("wi_raw", [P, 2, DC, COLW])
        w_hi = sb("wi_hi", [P, 2, DC, COLW], F32R)
        w_lo = sb("wi_lo", [P, 2, DC, COLW], F32R)
        ps = ctx.enter_context(nc.psum_tensor("ps_z", [P, 2, 2, HALF], F32))
        w_ld = [sem("wi_in0"), sem("wi_in1")]
        hi_done, lo_done, used, mm_done, copied = sem("wi_hi_done"), sem("wi_lo_done"), sem("wi_used"), sem("z_mm"), sem("z_copied")
        NG = 10
        block = ctx.enter_context(nc.Block())

        @block.sync
        def _(sp):
            for g in range(NG):
                if g >= 2:
                    sp.wait_ge(lo_done, g - 1)
                sp.dma_start(raw[:, g % 2], w_in[g]).then_inc(w_ld[g % 2], 16)

        @block.scalar
        def _(act):
            def split(g):
                act.wait_ge(w_ld[g % 2], 16 * (g // 2 + 1))
                if g >= 2:
                    act.wait_ge(used, g - 1)
                nc.scalar.activation(w_hi[:, g % 2], raw[:, g % 2], ACT.Copy).then_inc(hi_done, 1)

            split(0)
            split(1)
            for g in range(NG):
                for j in range(2 if g < 6 else 4):
                    m = 2 * g + j if g < 6 else 12 + 4 * (g - 6) + j
                    act.wait_ge(mm_done, m + 1)
                    if g < 6:
                        nc.scalar.activation(z_t[:, m], ps[:, j], ACT.Copy).then_inc(copied, 1)
                    else:
                        nc.scalar.activation(z_n[:, 2 * j:2 * j + 2, COLW * (g - 6):COLW * (g - 5)], ps[:, j % 2, :, 0:COLW],
                                             ACT.Copy).then_inc(copied, 1)
                if g + 2 < NG:
                    split(g + 2)

        @block.tensor
        def _(pe):
            passes = ((w_hi, h_hi), (w_hi, h_lo), (w_lo, h_hi))

            def features(w, b):
                pe.wait_ge(lo_done, 2 * w + b + 1)
                for j in range(2):
                    m = 4 * w + 2 * b + j
                    if not (isinstance(w, int) and b == 0):
                        pe.wait_ge(copied, m - 1)
                    for k in range(DC):
                        for i, (a, h) in enumerate(passes):
                            for half in range(2):
                                mm = pe.matmul(ps[:, j, half], a[:, b, k, j * P:j * P + P], h[:, k, half * HALF:half * HALF + HALF],
                                               start=(k == 0 and i == 0), stop=(k == DC - 1 and i == 2))
                    mm.then_inc(mm_done, 1)
                pe.wait_ge(mm_done, 4 * w + 2 * b + 2)
                pe.sem_inc(used, 1)

            def tokens(w, b):
                pe.wait_ge(lo_done, 2 * w + b + 7)
                for j in range(4):
                    m = 8 * w + 4 * b + j + 12
                    pe.wait_ge(copied, m - 1)
                    for a in range(2):
                        t = 2 * j + a
                        for k in range(DC):
                            for i, (wt, h) in enumerate(passes):
                                mm = pe.matmul(ps[:, j % 2, a, 0:COLW], h[:, k, t * P:t * P + P], wt[:, b, k],
                                               start=(k == 0 and i == 0), stop=(k == DC - 1 and i == 2))
                    mm.then_inc(mm_done, 1)
                pe.wait_ge(mm_done, 8 * w + 4 * b + 16)
                pe.sem_inc(used, 1)

            features(0, 0)
            features(0, 1)
            with loop(nc, pe, 1, 3) as w:
                features(w, 0)
                features(w, 1)
            with loop(nc, pe, 0, 2) as w:
                tokens(w, 0)
                tokens(w, 1)

        @block.vector
        def _(dve):
            for g in range(NG):
                dve.wait_ge(hi_done, g + 1)
                nc.vector.tensor_tensor(w_lo[:, g % 2], raw[:, g % 2], w_hi[:, g % 2].bitcast(F32), ALU.subtract).then_inc(lo_done, 1)


def mix(nc, z_t, z_n, sgu_wt, sgu_b, sgu_ln, lam_p, subln_col, rel_bias, bucket_hot, tbl_d, ident, cat_hi, cat_lo):
    with ExitStack() as ctx:
        sb = lambda n, s, d=F32: ctx.enter_context(nc.sbuf_tensor(n, s, d))
        sem = lambda n: ctx.enter_context(nc.semaphore("mx_" + n))
        wt = sb("sgu_w_t", [P, SGU_G, P])
        bt = sb("sgu_bias", [P, SGU_G // 2, P])
        ln_rows = sb("ln_rows", [P, 2, SW])
        stats = sb("ln_stats", [P, TT, 6])
        mv = sb("ln_mv", [P, TT, 2])
        lnr = sb("ln_root", [P, TT])
        lni = sb("ln_inv", [P, TT])
        eps = sb("eps_f3", [P, 1])
        rb = sb("rel_b", [RB, HEADS_A])
        rbb = sb("rel_bb", [RB, HEADS_A, P])
        hot = sb("hot", [RB, RLEN])
        far = sb("far_bias", [P, HEADS_A])
        far_pair = sb("far_pair", [P, 2])
        tb = sb("near_bias", [P, HEADS_A, 2 * P])
        lam = sb("lam_s", [P, 4, DH])
        lamw = sb("lam_w", [P, 2, DH])
        lamd = sb("lam_d", [P, 2])
        lame = sb("lam_e", [P, 2])
        neglam = sb("neg_lam", [P, 1])
        sg = sb("subln_in", [P, 1])
        sgs = sb("subln_scaled", [P, 1])
        logit = sb("logit", [P, 2, 2, S])
        att = sb("att", [P, 2, S])
        att_t = sb("att_t", [P, 2, TT, P])
        nmax = sb("nmax", [P, 2, 2])
        mx = sb("mx", [P, 2, 2])
        ssum = sb("ssum", [P, 2, 2])
        sinv = sb("sinv", [P, 2, 2])
        fac = sb("fac", [P, 2])
        osq = sb("osq", [P, TT, HEADS_A])
        ort = sb("ort", [P, TT, HEADS_A])
        oin = sb("oin", [P, TT, HEADS_A])
        ps_l = ctx.enter_context(nc.psum_tensor("ps_l", [P, 4, HALF], F32))
        ps_t = ctx.enter_context(nc.psum_tensor("ps_t", [P, TT, P], F32))
        ps_o = ctx.enter_context(nc.psum_tensor("ps_o", [P, 2, HALF], F32))
        o_all = z_n[:, :, 0:SW]
        pair_qk = z_t[:, 0:4]
        logit_row = logit[:].rearrange("p a b s -> p (a b s)")
        ps_row = ps_l[:].rearrange("p c s -> p (c s)")
        ps_far = ps_row[:, 0:3 * HALF].rearrange("p (c s) -> p c s", c=2)
        ps_near = ps_l[:, 3].rearrange("p (c s) -> p c s", c=2)

        w_ld, bt_ld, ln_ld, small_ld, tb_st, tb_ld = map(sem, "w_ld bt_ld ln_ld small_ld tb_st tb_ld".split())
        masked, tb_masked, ready, tb_mm, tb_copied, lam_exp = map(sem, "masked tb_masked ready tb_mm tb_copied lam_exp".split())
        gelu_v, gelu_u, agg, root, v_ready = map(sem, "gelu_v gelu_u agg root v_ready".split())
        mix_mm, mix_b, mix_u, sgu_hi, sgu_lo = map(sem, "mix_mm mix_b mix_u sgu_hi sgu_lo".split())
        pair_ready, l_half, l_done, near_done, far_done, max_done, exp_done = map(sem, "pair_ready l_half l_done near_done far_done max_done exp_done".split())
        comb_done, t_done, t_copied, o_mm, o_done, step = map(sem, "comb_done t_done t_copied o_mm o_done step".split())
        sq_sum, o_root, o_ready, ot_mm, o_scaled, o_hi, o_lo = map(sem, "sq_sum o_root o_ready ot_mm o_scaled o_hi o_lo".split())
        PAIR = 2 * TT
        FAR = [0]
        for m in range(PAIR):
            FAR.append(FAR[-1] + (m % TT >= 2))
        block = ctx.enter_context(nc.Block())

        @block.sync
        def _(sp):
            sp.dma_start(rb[:], rel_bias).then_inc(small_ld, 16)
            sp.dma_start(hot[:], bucket_hot).then_inc(small_ld, 16)
            sp.dma_start(lam[:].rearrange("p a b -> p (a b)"), lam_p.to_broadcast([P, 4 * DH])).then_inc(small_ld, 16)
            sp.dma_start(sg[:], subln_col).then_inc(small_ld, 16)
            for i in range(2):
                sp.dma_start(ln_rows[:, i], sgu_ln[i:i + 1].to_broadcast([P, SW])).then_inc(ln_ld, 16)
            sp.dma_start(wt[:], sgu_wt).then_inc(w_ld, 16)
            for half in range(2):
                src = sgu_b.rearrange("(a b) t -> b a t", b=2)[half:half + 1].to_broadcast([DH, SGU_G // 2, P])
                sp.dma_start(bt[half * DH:half * DH + DH], src).then_inc(bt_ld, 16)
            sp.wait_ge(tb_copied, HEADS_A)
            rows = logit_row[:, 0:HEADS_A * HALF].rearrange("p (h m) -> p h m", h=HEADS_A)
            sp.dma_start(tbl_d.rearrange("h p m -> p h m"), rows[:, :, 0:RLEN]).then_inc(tb_st, 16)
            sp.wait_ge(tb_st, 16)
            skew = bass.AP(tensor=tbl_d.tensor, offset=P - 1, ap=[[RLEN - 1, P], [P * RLEN, HEADS_A], [1, 2 * P]])
            sp.dma_start(tb[:], skew).then_inc(tb_ld, 16)

        @block.gpsimd
        def _(pool):
            pool.wait_ge(w_ld, 16)
            nc.gpsimd.affine_select(out=wt[:], in_=wt[:], compare_op=ALU.is_ge, fill=0.0, base=0,
                                    pattern=[[0, SGU_G], [1, P]], channel_multiplier=-1).then_inc(masked, 1)
            pool.wait_ge(tb_ld, 16)
            nc.gpsimd.affine_select(out=tb[:], in_=tb[:], compare_op=ALU.is_ge, fill=LOWEST, base=P,
                                    pattern=[[0, HEADS_A], [-1, 2 * P]], channel_multiplier=1).then_inc(tb_masked, 1)

        @block.scalar
        def _(act):
            for h in range(HEADS_A):
                act.wait_ge(tb_mm, HEADS_A)
                nc.scalar.activation(logit_row[:, h * HALF:h * HALF + RLEN], ps_row[:, h * HALF:h * HALF + RLEN],
                                     ACT.Copy).then_inc(tb_copied, 1)
            act.wait_ge(ready, 2)
            nc.scalar.activation(lame[:], lamd[:], ACT.Exp).then_inc(lam_exp, 1)
            for t in range(TT):
                nc.scalar.activation(z_n[:, t, 0:SW], z_n[:, t, 0:SW], ACT.Gelu_apprx_tanh).then_inc(gelu_v, 1)
            for c in range(4):
                nc.scalar.activation(z_t[:, c], z_t[:, c], ACT.Gelu_apprx_tanh).then_inc(gelu_u, 1)
            act.wait_ge(agg, TT)
            nc.scalar.activation(lnr[:], mv[:, :, 1], ACT.Sqrt, bias=eps[:]).then_inc(root, 1)
            for c in range(TT):
                act.wait_ge(mix_u, c + 1)
                nc.scalar.activation(cat_hi[:, 0:4, c * P:c * P + P], att[:, c % 2, 0:SW].rearrange("p (g t) -> p g t", g=4),
                                     ACT.Copy).then_inc(sgu_hi, 1)

            def far_part(w, m):
                i = m % TT
                if i < 2:
                    return
                n = (i - 1) * P
                act.wait_ge(l_done, PAIR * w + m + 1)
                act.wait_ge(comb_done, PAIR * w + m - 1)
                nc.scalar.activation(logit[:, m % 2, :, 0:n], ps_far[:, :, 0:n], ACT.Identity,
                                     bias=far_pair[:, m // TT:m // TT + 1]).then_inc(far_done, 1)

            def exps(w, m):
                n = (m % TT + 1) * P
                act.wait_ge(max_done, PAIR * w + m + 1)
                for c in range(2):
                    nc.scalar.activation(logit[:, m % 2, c, 0:n], logit[:, m % 2, c, 0:n], ACT.Exp, bias=nmax[:, m % 2, c:c + 1],
                                         accum_out=ssum[:, m % 2, c:c + 1]).then_inc(exp_done, 1)

            def copy_t(w, m):
                n = m % TT + 1
                act.wait_ge(t_done, PAIR * w + m + 1)
                act.wait_ge(o_mm, PAIR * w + max(m - 1, 0))
                nc.scalar.activation(att_t[:, m % 2, 0:n], ps_t[:, 0:n], ACT.Copy).then_inc(t_copied, 1)

            with loop(nc, act, 0, HEADS_A // 2) as w:
                exps(w, 0)
                for m in range(PAIR):
                    if m + 1 < PAIR:
                        far_part(w, m + 1)
                    copy_t(w, m)
                    if m + 1 < PAIR:
                        exps(w, m + 1)
            act.wait_ge(sq_sum, 2)
            nc.scalar.activation(ort[:], osq[:], ACT.Sqrt, bias=eps[:], scale=1.0 / VD).then_inc(o_root, 1)
            for t in range(TT):
                act.wait_ge(ot_mm, t + 1)
                if t >= 2:
                    act.wait_ge(o_lo, t - 1)
                nc.scalar.activation(att[:, t % 2, 0:SW], ps_l[:, t % 2, 0:SW], ACT.Copy, scale=sgs[:]).then_inc(o_scaled, 1)
                act.wait_ge(o_scaled, t + 1)
                nc.scalar.activation(cat_hi[:, 4:8, t * P:t * P + P], att[:, t % 2, 0:SW].rearrange("p (g t) -> p g t", g=4),
                                     ACT.Copy).then_inc(o_hi, 1)

        @block.tensor
        def _(pe):
            pe.wait_ge(ready, 4)
            for h in range(HEADS_A):
                mm = pe.matmul(ps_row[:, h * HALF:h * HALF + RLEN], rbb[:, h], hot[:], start=True, stop=True)
            mm.then_inc(tb_mm, HEADS_A)
            pe.wait_ge(tb_copied, HEADS_A)
            pe.wait_ge(masked, 1)
            pe.wait_ge(v_ready, 1)
            for c in range(TT):
                if c >= 2:
                    pe.wait_ge(mix_b, c - 1)
                for g in range(SGU_G):
                    r = g % 2 * DH
                    mm = pe.matmul(ps_l[r:r + DH, c % 2, g // 2 * P:g // 2 * P + P], z_n[:, c, g * DH:g * DH + DH], wt[:, g],
                                   start=True, stop=True)
                mm.then_inc(mix_mm, 1)

            def logits(w, m):
                g = PAIR * w + m
                hh, i = m // TT, m % TT
                if m == 0:
                    pe.wait_ge(pair_ready, 3 * w + 3)
                pe.wait_ge(near_done, g)
                pe.wait_ge(far_done, FAR[PAIR] * w + FAR[m])
                split = max(i - 1, 0) * P
                for c in range(2):
                    cuts = [0, HALF if c == 0 else HALF // 2, split]
                    parts = [(ps_far[:, c, k0:min(k1, split)], k0, min(k1, split)) for k0, k1 in zip(cuts, cuts[1:]) if k0 < split]
                    parts.append((ps_near[:, c, 0:(i + 1) * P - split], split, (i + 1) * P))
                    for dst, k0, k1 in parts:
                        mm = pe.matmul(dst, pair_qk[c * DH:c * DH + DH, hh, i * P:i * P + P],
                                       pair_qk[c * DH:c * DH + DH, 2 + hh, k0:k1], start=True, stop=True)
                    if c == 0:
                        mm.then_inc(l_half, 1)
                        pe.wait_ge(l_half, g + 1)
                mm.then_inc(l_done, 1)

            def turn(w, m):
                pe.wait_ge(comb_done, PAIR * w + m + 1)
                pe.wait_ge(t_copied, PAIR * w + m)
                for j in range(m % TT + 1):
                    mm = pe.transpose(ps_t[:, j], att[:, m % 2, j * P:j * P + P], ident[:])
                mm.then_inc(t_done, 1)

            def values(w, m):
                i = m % TT
                pe.wait_ge(t_copied, PAIR * w + m + 1)
                pe.wait_ge(o_done, PAIR * w + max(m - 1, 0))
                col = SW + (2 * w + m // TT) * VD
                for j in range(i + 1):
                    mm = pe.matmul(ps_o[:, m % 2, 0:VD], att_t[:, m % 2, j], z_n[:, j, bass.ds(col, VD)],
                                   start=(j == 0), stop=(j == i))
                mm.then_inc(o_mm, 1)

            pe.wait_ge(mix_b, TT)
            with loop(nc, pe, 0, HEADS_A // 2) as w:
                logits(w, 0)
                for m in range(PAIR):
                    if m + 1 < PAIR:
                        logits(w, m + 1)
                    turn(w, m)
                    if m >= 1:
                        values(w, m - 1)
                values(w, PAIR - 1)
            pe.wait_ge(o_ready, 1)
            for t in range(TT):
                if t >= 2:
                    pe.wait_ge(o_scaled, t - 1)
                for h in range(HEADS_A):
                    mm = pe.transpose(ps_l[:, t % 2, h * P:h * P + P], o_all[:, t, h * VD:h * VD + VD], ident[:])
                mm.then_inc(ot_mm, 1)

        @block.vector
        def _(dve):
            ch = Chain(dve, step)
            nc.vector.memset(eps[:], EPS).then_inc(ready, 1)
            dve.wait_ge(small_ld, 64)
            nc.vector.tensor_copy(rbb[:], rb[:].unsqueeze(2).to_broadcast([RB, HEADS_A, P])).then_inc(ready, 1)
            ch.done(nc.vector.tensor_tensor(lamw[:], lam[:, 0:4:2], lam[:, 1:4:2], ALU.mult))
            ch.sync()
            nc.vector.tensor_reduce(lamd[:], lamw[:], AX.X, ALU.add).then_inc(ready, 1)
            nc.vector.tensor_scalar(sgs[:], sg[:], 1.0 - LAM_INIT, None, ALU.mult).then_inc(ready, 1)
            dve.wait_ge(lam_exp, 1)
            ch.done(nc.vector.scalar_tensor_tensor(out=neglam[:], in0=lame[:, 1:2], scalar=-LAM_INIT, in1=lame[:, 0:1],
                                                   op0=ALU.add, op1=ALU.subtract))
            dve.wait_ge(tb_copied, HEADS_A)
            ch.done(nc.vector.tensor_copy(far[:], logit_row[:, 0:HEADS_A * HALF:HALF]))
            for t in range(TT):
                dve.wait_ge(gelu_v, t + 1)
                ch.done(nc.vector.bn_stats(stats[:, t], z_n[:, t, 0:SW]))
            for t in range(TT):
                ch.sync(TT - 1 - t)
                nc.vector.bn_aggr(mv[:, t], stats[:, t]).then_inc(agg, 1)
            dve.wait_ge(root, 1)
            ch.done(nc.vector.reciprocal(lni[:], lnr[:]))
            ch.sync()
            for t in range(TT):
                ch.done(nc.vector.tensor_scalar(z_n[:, t, 0:SW], z_n[:, t, 0:SW], mv[:, t, 0:1], lni[:, t:t + 1],
                                                ALU.subtract, ALU.mult))
            ch.sync()
            dve.wait_ge(ln_ld, 32)
            v = z_n[:, :, 0:SW]
            ch.done(nc.vector.tensor_tensor(v, v, ln_rows[:, 0].unsqueeze(1).to_broadcast([P, TT, SW]), ALU.mult))
            ch.sync()
            nc.vector.tensor_tensor(v, v, ln_rows[:, 1].unsqueeze(1).to_broadcast([P, TT, SW]), ALU.add).then_inc(v_ready, 1)
            dve.wait_ge(bt_ld, 32)
            dve.wait_ge(gelu_u, 4)
            for c in range(TT):
                a = att[:, c % 2, 0:SW].rearrange("p (g t) -> p g t", g=4)
                dve.wait_ge(mix_mm, c + 1)
                if c >= 2:
                    dve.wait_ge(sgu_lo, c - 1)
                nc.vector.tensor_tensor(a, ps_l[:, c % 2, 0:SW].rearrange("p (g t) -> p g t", g=4), bt[:], ALU.add).then_inc(mix_b, 1)
                dve.wait_ge(mix_b, c + 1)
                nc.vector.tensor_tensor(a, a, z_t[:, 0:4, c * P:c * P + P], ALU.mult).then_inc(mix_u, 1)
                dve.wait_ge(sgu_hi, c + 1)
                nc.vector.tensor_tensor(cat_lo[:, 0:4, c * P:c * P + P], a, cat_hi[:, 0:4, c * P:c * P + P].bitcast(F32),
                                        ALU.subtract).then_inc(sgu_lo, 1)
            dve.wait_ge(sgu_lo, TT)
            dve.wait_ge(tb_masked, 1)
            dve.wait_ge(tb_st, 16)
            ch.sync()

            def near(w, m):
                i = m % TT
                k0, width = (i - 1) * P if i else 0, 2 * P if i else P
                dve.wait_ge(l_done, PAIR * w + m + 1)
                dve.wait_ge(comb_done, PAIR * w + max(m - 1, 0))
                bias = tb[:, bass.ds(2 * w + m // TT, 1), 2 * P - width:2 * P].to_broadcast([P, 2, width])
                nc.vector.tensor_tensor(logit[:, m % 2, :, k0:k0 + width], ps_near[:, :, 0:width], bias, ALU.add).then_inc(near_done, 1)

            def maximum(w, m):
                g = PAIR * w + m
                n = (m % TT + 1) * P
                dve.wait_ge(near_done, g + 1)
                dve.wait_ge(far_done, FAR[PAIR] * w + FAR[m + 1])
                ch.done(nc.vector.tensor_reduce(mx[:, m % 2], logit[:, m % 2, :, 0:n], AX.X, ALU.max))
                ch.sync()
                nc.vector.tensor_scalar(nmax[:, m % 2], mx[:, m % 2], -1.0, None, ALU.mult).then_inc(max_done, 1)

            def combine(w, m):
                g = PAIR * w + m
                n = (m % TT + 1) * P
                b = m % 2
                dve.wait_ge(exp_done, 2 * g + 2)
                dve.wait_ge(o_done, PAIR * w + max(m - 1, 0))
                ch.done(nc.vector.reciprocal(sinv[:, b], ssum[:, b]))
                ch.sync()
                ch.done(nc.vector.scalar_tensor_tensor(out=fac[:, b:b + 1], in0=ssum[:, b, 0:1], scalar=neglam[:], in1=sinv[:, b, 1:2],
                                                       op0=ALU.mult, op1=ALU.mult))
                ch.sync()
                dve.wait_ge(t_done, PAIR * w + max(m - 1, 0))
                nc.vector.scalar_tensor_tensor(out=att[:, b, 0:n], in0=logit[:, b, 1, 0:n], scalar=fac[:, b:b + 1],
                                               in1=logit[:, b, 0, 0:n], op0=ALU.mult, op1=ALU.add).then_inc(comb_done, 1)

            def output(w, m):
                dve.wait_ge(o_mm, PAIR * w + m + 1)
                col = (2 * w + m // TT) * VD
                nc.vector.tensor_scalar(o_all[:, m % TT, bass.ds(col, VD)], ps_o[:, m % 2, 0:VD], sinv[:, m % 2, 0:1], None,
                                        ALU.mult).then_inc(o_done, 1)

            ch.reset()
            with loop(nc, dve, 0, HEADS_A // 2) as w:
                dve.wait_ge(l_done, PAIR * w)
                dve.wait_ge(far_done, FAR[PAIR] * w)
                nc.vector.tensor_scalar(pair_qk[:, 0:2], z_t[:, bass.ds(4 + 2 * w, 2)], DH ** -0.5, None, ALU.mult).then_inc(pair_ready, 1)
                nc.vector.tensor_copy(pair_qk[:, 2:4], z_t[:, bass.ds(8 + 2 * w, 2)]).then_inc(pair_ready, 1)
                nc.vector.tensor_copy(far_pair[:], far[:, bass.ds(2 * w, 2)]).then_inc(pair_ready, 1)
                near(w, 0)
                maximum(w, 0)
                for m in range(PAIR):
                    if m + 1 < PAIR:
                        near(w, m + 1)
                    combine(w, m)
                    if m + 1 < PAIR:
                        maximum(w, m + 1)
                    if m >= 1:
                        output(w, m - 1)
                output(w, PAIR - 1)
                ch.reset()
            dve.wait_ge(o_done, HEADS_A * TT)
            big = logit_row[:, 0:TT * SW].rearrange("p (t n) -> p t n", t=TT)
            nc.vector.tensor_tensor(big, o_all, o_all, ALU.mult).then_inc(sq_sum, 1)
            dve.wait_ge(sq_sum, 1)
            nc.vector.tensor_reduce(osq[:], big.rearrange("p t (h n) -> p t h n", h=HEADS_A), AX.X, ALU.add).then_inc(sq_sum, 1)
            dve.wait_ge(o_root, 1)
            ch.done(nc.vector.reciprocal(oin[:], ort[:]))
            ch.sync()
            o4 = o_all.rearrange("p t (h n) -> p t h n", h=HEADS_A)
            nc.vector.tensor_tensor(o4, o4, oin[:].unsqueeze(3).to_broadcast([P, TT, HEADS_A, VD]), ALU.mult).then_inc(o_ready, 1)
            for t in range(TT):
                dve.wait_ge(o_hi, t + 1)
                nc.vector.tensor_tensor(cat_lo[:, 4:8, t * P:t * P + P], att[:, t % 2, 0:SW].rearrange("p (g t) -> p g t", g=4),
                                        cat_hi[:, 4:8, t * P:t * P + P].bitcast(F32), ALU.subtract).then_inc(o_lo, 1)


def out_project_and_norm(nc, x, w_out, h_hi, h_lo, mod_cols, gain1, ident, x_mid):
    with ExitStack() as ctx:
        sb = lambda n, s, d=F32: ctx.enter_context(nc.sbuf_tensor(n, s, d))
        sem = lambda n: ctx.enter_context(nc.semaphore("op_" + n))
        raw = sb("wo_raw", [P, 2, D])
        w_hi = sb("wo_hi", [P, DC, D], F32R)
        w_lo = sb("wo_lo", [P, DC, D], F32R)
        xt = sb("x_in_rows", [P, 2, D])
        xm = sb("x_mid_rows", [P, 2, D])
        xr = sb("x_mid_scaled", [P, 2, D])
        hf = sb("h2_full", [P, 2, DC, P])
        sq_out = sb("squares_y", [P, 2, HALF])
        sq_out2 = sb("squares_x", [P, D])
        ssy, rty, iny = sb("ssy", [P, TT]), sb("rty", [P, TT]), sb("iny", [P, TT])
        ssx, rtx, inx = sb("ssx", [P, TT]), sb("rtx", [P, TT]), sb("inx", [P, TT])
        eps = sb("eps_f4", [P, 1])
        ps_y = ctx.enter_context(nc.psum_tensor("ps_yo", [P, 2, 2, HALF], F32))
        ps_x = ctx.enter_context(nc.psum_tensor("ps_xo", [P, 2, DC, P], F32))
        w_ld = [sem("w_ld0"), sem("w_ld1")]
        x_ld = [sem("x_ld0"), sem("x_ld1")]
        x_st = [sem("x_st0"), sem("x_st1")]
        w_hid, w_lod, y_mm, ysq, yrt, yin, y_gain, x_new = map(sem, "w_hi w_lo y_mm ysq yrt yin y_gain x_new".split())
        xsq, xrt, xin, xr_done, xt_done, hf_done, hi_done, lo_done, ready = map(sem, "xsq xrt xin xr xt hf hi lo ready".split())
        block = ctx.enter_context(nc.Block())

        @block.sync
        def _(sp):
            for k in range(DC):
                if k >= 2:
                    sp.wait_ge(w_lod, k - 1)
                sp.dma_start(raw[:, k % 2], w_out[:, k]).then_inc(w_ld[k % 2], 16)
            for t in range(TT):
                if t >= 2:
                    sp.wait_ge(x_new, t - 1)
                sp.dma_start(xt[:, t % 2], x[t * P:t * P + P]).then_inc(x_ld[t % 2], 16)
                if t >= 1:
                    sp.wait_ge(x_new, t)
                    sp.dma_start(x_mid[t * P - P:t * P], xm[:, (t - 1) % 2]).then_inc(x_st[(t - 1) % 2], 16)
            sp.wait_ge(x_new, TT)
            sp.dma_start(x_mid[S - P:S], xm[:, 1]).then_inc(x_st[1], 16)
            for b in range(2):
                sp.wait_ge(x_st[b], 16 * TT // 2)

        @block.scalar
        def _(act):
            for k in range(DC):
                act.wait_ge(w_ld[k % 2], 16 * (k // 2 + 1))
                nc.scalar.activation(w_hi[:, k], raw[:, k % 2], ACT.Copy).then_inc(w_hid, 1)
            act.wait_ge(ready, 1)

            def y_root(t):
                act.wait_ge(y_mm, t + 1)
                if t >= 1:
                    act.wait_ge(ysq, t)
                nc.scalar.activation(sq_out[:], ps_y[:, t % 2], ACT.Square, accum_out=ssy[:, t:t + 1]).then_inc(ysq, 1)
                act.wait_ge(ysq, t + 1)
                nc.scalar.activation(rty[:, t:t + 1], ssy[:, t:t + 1], ACT.Sqrt, bias=eps[:], scale=1.0 / D).then_inc(yrt, 1)

            def x_root(t):
                act.wait_ge(x_new, t + 1)
                if t >= 1:
                    act.wait_ge(xsq, t)
                nc.scalar.activation(sq_out2[:], xm[:, t % 2], ACT.Square, accum_out=ssx[:, t:t + 1]).then_inc(xsq, 1)
                act.wait_ge(xsq, t + 1)
                nc.scalar.activation(rtx[:, t:t + 1], ssx[:, t:t + 1], ACT.Sqrt, bias=eps[:], scale=1.0 / D).then_inc(xrt, 1)

            def hi(t):
                act.wait_ge(hf_done, 2 * t + 2)
                nc.scalar.activation(h_hi[:, :, t * P:t * P + P], hf[:, t % 2], ACT.Copy).then_inc(hi_done, 1)

            for t in range(TT):
                y_root(t)
                if t >= 1:
                    hi(t - 1)
                x_root(t)
            hi(TT - 1)

        @block.tensor
        def _(pe):
            pe.wait_ge(w_lod, DC)

            def project(t):
                if t >= 2:
                    pe.wait_ge(y_gain, t - 1)
                for k in range(DC):
                    for i, (c, w) in enumerate(((h_hi, w_hi), (h_hi, w_lo), (h_lo, w_hi))):
                        for half in range(2):
                            mm = pe.matmul(ps_y[:, t % 2, half], c[:, k, t * P:t * P + P], w[:, k, half * HALF:half * HALF + HALF],
                                           start=(k == 0 and i == 0), stop=(k == DC - 1 and i == 2))
                mm.then_inc(y_mm, 1)

            def turn(t):
                pe.wait_ge(xr_done, t + 1)
                if t >= 2:
                    pe.wait_ge(hf_done, 2 * (t - 2) + 1)
                for k in range(DC):
                    mm = pe.transpose(ps_x[:, t % 2, k], xr[:, t % 2, k * P:k * P + P], ident[:])
                mm.then_inc(xt_done, 1)

            for t in range(TT):
                project(t)
                if t >= 1:
                    turn(t - 1)
            turn(TT - 1)

        @block.vector
        def _(dve):
            nc.vector.memset(eps[:], EPS).then_inc(ready, 1)
            for k in range(DC):
                dve.wait_ge(w_hid, k + 1)
                nc.vector.tensor_tensor(w_lo[:, k], raw[:, k % 2], w_hi[:, k].bitcast(F32), ALU.subtract).then_inc(w_lod, 1)

            def residual(t):
                b = t % 2
                dve.wait_ge(yrt, t + 1)
                nc.vector.reciprocal(iny[:, t:t + 1], rty[:, t:t + 1]).then_inc(yin, 1)
                dve.wait_ge(yin, t + 1)
                if t >= 2:
                    dve.wait_ge(x_st[b], 16 * (t // 2))
                    dve.wait_ge(xr_done, t - 1)
                    dve.wait_ge(xsq, t - 1)
                nc.vector.scalar_tensor_tensor(out=xm[:, b], in0=ps_y[:, b].rearrange("p a b -> p (a b)"), scalar=iny[:, t:t + 1],
                                               in1=gain1[:], op0=ALU.mult, op1=ALU.mult).then_inc(y_gain, 1)
                dve.wait_ge(y_gain, t + 1)
                dve.wait_ge(x_ld[b], 16 * (t // 2 + 1))
                nc.vector.tensor_tensor(xm[:, b], xm[:, b], xt[:, b], ALU.add).then_inc(x_new, 1)

            def scaled(t):
                b = t % 2
                dve.wait_ge(xrt, t + 1)
                nc.vector.reciprocal(inx[:, t:t + 1], rtx[:, t:t + 1]).then_inc(xin, 1)
                dve.wait_ge(xin, t + 1)
                if t >= 2:
                    dve.wait_ge(xt_done, t - 1)
                nc.vector.tensor_scalar(xr[:, b], xm[:, b], inx[:, t:t + 1], None, ALU.mult).then_inc(xr_done, 1)

            def modulated(t):
                dve.wait_ge(xt_done, t + 1)
                if t >= 2:
                    dve.wait_ge(lo_done, t - 1)
                    dve.wait_ge(hi_done, t - 1)
                affine_cols(nc, dve, hf[:, t % 2], ps_x[:, t % 2], mod_cols[:, 2], mod_cols[:, 3], hf_done, 2 * t)
                dve.wait_ge(hi_done, t + 1)
                nc.vector.tensor_tensor(h_lo[:, :, t * P:t * P + P], hf[:, t % 2], h_hi[:, :, t * P:t * P + P].bitcast(F32),
                                        ALU.subtract).then_inc(lo_done, 1)

            for t in range(TT):
                residual(t)
                if t >= 1:
                    modulated(t - 1)
                scaled(t)
            modulated(TT - 1)


def layout(d):
    import numpy as np
    L = {}
    L["x"] = d["x"][0]
    L["c_col"] = d["c"].reshape(DC, P).T
    L["w_ada"] = d["w_ada"][0].reshape(DC, P, NADA, D).transpose(2, 0, 1, 3)
    L["b_ada"] = d["b_ada"]
    L["norm_g"] = d["norm_g"][0]
    L["g_col"] = d["norm_g"][0].reshape(4, DC, P).transpose(2, 0, 1)
    w = d["w_in"][0].reshape(DC, P, 10, COLW).transpose(2, 1, 0, 3)
    L["w_in"] = w[[0, 1, 4, 5, 6, 7, 2, 3, 8, 9]]
    L["sgu_wt"] = d["sgu_w"][0].transpose(2, 0, 1)
    L["sgu_b"] = d["sgu_b"][0]
    L["sgu_ln"] = np.concatenate([d["sgu_ln_g"], d["sgu_ln_b"]])
    L["lam_p"] = d["diff_lambda"].reshape(1, 4 * DH)
    L["subln_col"] = d["diff_subln_g"].reshape(VD, 1)
    L["rel_bias"] = d["rel_bias"]
    n = np.maximum(255 - np.arange(RLEN), 0)
    exact = RB // 2
    big = exact + (np.log(np.maximum(n, 1).astype(np.float32) / exact) / math.log(128 / exact) * (RB - exact)).astype(np.int32)
    bucket = np.where(n < exact, n, np.minimum(big, RB - 1))
    L["bucket_hot"] = (np.arange(RB)[:, None] == bucket[None]).astype(np.float32)
    L["w_out"] = d["w_out"][0].reshape(DC, P, D).transpose(1, 0, 2)
    cols = np.empty((NQ + ETILES, P, DC, P), d["peer_u"].dtype)
    cols[:NQ] = d["peer_w_query"][0].reshape(DC, P, NQ, P).transpose(2, 1, 0, 3)
    cols[NQ:] = d["peer_u"][0].reshape(P, ETILES, DC, P).transpose(1, 3, 2, 0)
    L["cols"] = cols
    L["keys_t"] = d["peer_sub_keys"][0].transpose(3, 0, 1, 2).reshape(P, HC, NKEY)
    L["v_cols"] = d["peer_v"][0].reshape(P, ETILES, D).transpose(1, 0, 2)
    return {k: np.ascontiguousarray(v) for k, v in L.items()}


def build(nc, t, scratch="Internal"):
    dram = lambda n, s: nc.dram_tensor(n, s, F32, kind=scratch).ap()
    x_mid = dram("x_mid", (S, D))
    tbl = dram("distance_rows", (HEADS_A, P, RLEN))
    scores = dram("scores", (TT, HEADS, P, 2, NKEY))
    act_d = dram("expert_act", (ETILES, P, S))
    gate_d = dram("expert_gate", (S // GBLK, P, ETILES, GBLK))
    with ExitStack() as ctx:
        sb = lambda n, s, d=F32: ctx.enter_context(nc.sbuf_tensor(n, s, d))
        gain2 = sb("gain2", [P, D])
        with ExitStack() as inner:
            sb = lambda n, s, d=F32: inner.enter_context(nc.sbuf_tensor(n, s, d))
            h_hi = sb("h_hi", [P, DC, S], F32R)
            h_lo = sb("h_lo", [P, DC, S], F32R)
            with ExitStack() as front:
                sb = lambda n, s, d=F32: front.enter_context(nc.sbuf_tensor(n, s, d))
                ident = sb("ident_f", [P, P])
                mod_cols = sb("mod_cols", [P, 4, DC])
                gain1 = sb("gain1", [P, D])
                modulate_and_norm(nc, t["x"], t["c_col"], t["w_ada"], t["b_ada"], t["norm_g"], t["g_col"], ident,
                                  h_hi, h_lo, mod_cols, gain1, gain2)
                with nc.sbuf_tensor("z_t", [P, 12, S], F32) as z_t, nc.sbuf_tensor("z_n", [P, TT, 2 * SW], F32) as z_n:
                    in_project(nc, t["w_in"], h_hi, h_lo, z_t, z_n)
                    mix(nc, z_t, z_n, t["sgu_wt"], t["sgu_b"], t["sgu_ln"], t["lam_p"], t["subln_col"], t["rel_bias"],
                        t["bucket_hot"], tbl, ident, h_hi, h_lo)
                out_project_and_norm(nc, t["x"], t["w_out"], h_hi, h_lo, mod_cols, gain1, ident, x_mid)
            route_and_up(nc, h_hi, h_lo, t["cols"], t["keys_t"], scores, act_d, gate_d)
        down_and_finish(nc, act_d, gate_d, t["v_cols"], x_mid, gain2, t["out"])


def kernel(**inputs):
    import concourse.bacc as bacc
    from concourse.bass_utils import run_bass_kernel_spmd

    arrays = layout({k: np.asarray(v) for k, v in inputs.items()})
    nc = bacc.Bacc("TRN2", target_bir_lowering=False, num_devices=1)
    t = {k: nc.dram_tensor(k, v.shape, mybir.dt.from_np(v.dtype), kind="ExternalInput").ap() for k, v in arrays.items()}
    t["out"] = nc.dram_tensor("out", (S, D), F32, kind="ExternalOutput").ap()
    build(nc, t)
    r = run_bass_kernel_spmd(nc, [arrays], core_ids=[0])
    return r.results[0]["out"].reshape(1, S, D)
```

```python
import math

import concourse.bass as bass
from concourse import mybir
from contextlib import ExitStack
import numpy as np

F32 = mybir.dt.float32
F32R = mybir.dt.float32r
U32 = mybir.dt.uint32
I32 = mybir.dt.int32
ALU = mybir.AluOpType
ACT = mybir.ActivationFunctionType
AX = mybir.AxisListType

P = 128
D = 1024
DC = D // P
S = 1024
TT = S // P
HALF = 512
HEADS = 8
TOPK = 16
NKEY = 128
HC = 2 * HEADS
ETILES = NKEY
NQ = HC
LOWEST = -3.0e38
GT = 8
GBLK = 32
EPS = 1e-6


class Chain:

    def __init__(self, eng, sem):
        self.eng, self.sem, self.n = eng, sem, 0

    def done(self, ins):
        self.n += 1
        return ins.then_inc(self.sem, 1)

    def sync(self, back=0):
        if self.n - back > 0:
            self.eng.wait_ge(self.sem, self.n - back)

    def reset(self):
        self.sync()
        self.eng.sem_clear(self.sem)
        self.n = 0


def loop(nc, eng, start, end):
    return nc.Fori(start, end, engines=[eng.engine], hint_back_edge=True)


def route_and_up(nc, h_hi, h_lo, stage, columns, ident, cols, keys_t, v_cols, v_in, a_in, scores, act_d, gate_d):
    with ExitStack() as ctx:
        sb = lambda n, s, d=F32: ctx.enter_context(nc.sbuf_tensor(n, s, d))
        sem = lambda n: ctx.enter_context(nc.semaphore(n))
        raw, c_hi, c_lo = columns.raw, columns.hi, columns.lo
        res = stage[:, 0:2 * S].rearrange("p (b t) -> p b t", b=2)
        keys = sb("keys", [P, HC, NKEY])
        sc_out = sb("sc_out", [P, 2, TT, NKEY])
        sc_in = sb("sc_in", [P, 2, 2, NKEY])
        first_hot = sb("first_hot", [P, 2, GT, NKEY], F32R)
        second_hot = sb("second_hot", [P, 2, GT, NKEY])
        second_gate = sb("second_gate", [P, 2, GT, 2, NKEY], F32R)
        g_buf = sb("g_buf", [P, ETILES, GBLK])
        iota = sb("iota", [P, NKEY])
        iota_i = sb("iota_i", [P, NKEY], I32)
        work = sb("work", [P, 2, NKEY])
        top = sb("top", [P, 2, TOPK])
        topi = sb("topi", [P, 2, TOPK], U32)
        topf = sb("topf", [P, 2, TOPK])
        cand = sb("cand", [P, TOPK, TOPK])
        cand2 = sb("cand2", [P, TOPK, TOPK])
        best = sb("best", [P, TOPK])
        pos = sb("pos", [P, TOPK], U32)
        pos2 = sb("pos2", [P, 2, TOPK], U32)
        pick = sb("pick", [P, 2, TOPK, TOPK])
        pick2 = sb("pick2", [P, 2, TOPK, TOPK])
        idx = sb("idx", [P, 2, HEADS * TOPK])
        shifted = sb("shifted", [P, HEADS * TOPK])
        expd = sb("expd", [P, HEADS, TOPK])
        esum = sb("esum", [P, HEADS])
        einv = sb("einv", [P, HEADS])
        rt = sb("rt", [P, 3, P])
        idx_t = sb("idx_t", [P, 2, P])
        gate_hi = sb("gate_hi", [P, P], F32R)
        gate_lo = sb("gate_lo", [P, P], F32R)
        ps_up = columns.ps
        ps_g = ctx.enter_context(nc.psum_tensor("ps_g", [P, GT, 2, NKEY], F32))
        ps_s = ps_g[:].rearrange("p (c t) h n -> p c (t h) n", c=2)

        keys_in = sem("keys_in")
        raw_in, hi_done, lo_done = columns.loaded, columns.hi_done, columns.lo_done
        up_done, res_done = sem("up_done"), sem("res_done")
        res_out = [sem("res_out0"), sem("res_out1")]
        sc_mm, sc_copied = sem("sc_mm"), sem("sc_copied")
        sc_stored = [sem("sc_stored0"), sem("sc_stored1")]
        sc_loaded = [sem("sc_loaded0"), sem("sc_loaded1")]
        head_read = sem("head_read")
        tile_routed, exp_done, gates_done = sem("tile_routed"), sem("exp_done"), sem("gates_done")
        turned, turn_copied = sem("turned"), sem("turn_copied")
        eq_ready, q_ready, p_ready = sem("eq_ready"), sem("q_ready"), sem("p_ready")
        g_done, g_half, g_copied, g_stored = sem("g_done"), sem("g_half"), sem("g_copied"), sem("g_stored")
        consts = sem("consts")
        dve_step = sem("dve_step")
        last_n = NQ + ETILES - 1

        def isint(x):
            return isinstance(x, int)

        block = ctx.enter_context(nc.Block())

        def supersteps(eng, quarter):
            def token_tile(s):
                quarter(s, 0)
                with loop(nc, eng, 1, 4) as v:
                    quarter(s, v)

            token_tile(0)
            with loop(nc, eng, 1, TT - 1) as s:
                token_tile(s)
            quarter(TT - 1, 0)
            with loop(nc, eng, 1, 3) as v:
                quarter(TT - 1, v)
            quarter(TT - 1, 3)

        @block.sync
        def _(sp):
            sp.dma_start(raw[:, 0], cols[2]).then_inc(raw_in[0], 16)
            sp.dma_start(keys[:], keys_t).then_inc(keys_in, 16)

            def load_ahead(n, b):
                sp.wait_ge(lo_done, n + 2)
                nxt = cols[n + 3] if isint(n) else cols[bass.ds(n + 3, 1)].rearrange("o p c n -> (o p) c n")
                sp.dma_start(raw[:, 1 - b], nxt).then_inc(raw_in[1 - b], 16)

            with loop(nc, sp, 0, HEADS) as u:
                load_ahead(2 * u, 0)
                load_ahead(2 * u + 1, 1)
                for c in range(2):
                    sp.wait_ge(sc_copied, 2 * u + c + 1)
                    dst = scores[:, bass.ds(u, 1), :, c, :].rearrange("a h t n -> t (a h) n")
                    sp.dma_start(dst, sc_out[:, c]).then_inc(sc_stored[c], 16)
            for c in range(2):
                sp.wait_ge(sc_stored[c], 16 * HEADS)

            def gates_out(blk):
                sp.wait_ge(g_copied, 4 * blk + 4)
                sp.dma_start(gate_d[bass.ds(blk, 1)].rearrange("o p j t -> (o p) j t"), g_buf[:]).then_inc(g_stored, 16)

            def quarter(s, v):
                last = isint(v) and v == 3
                if not (isint(s) and s == TT - 1):
                    for j in range(2):
                        sp.wait_ge(head_read, 8 * s + 2 * v + j + HEADS - 1)
                        src = scores[bass.ds(s + 1, 1), bass.ds(2 * v + j, 1)].rearrange("a h t c n -> (a h t) c n")
                        sp.dma_start(sc_in[:, j], src).then_inc(sc_loaded[j], 16)
                for q in range(4):
                    e = 16 * s + 4 * v + q
                    n = e + NQ
                    if not isint(n) or n + 3 <= last_n:
                        load_ahead(n, q % 2)
                    if last and q == 3:
                        gates_out(4 * s + v)
                    sp.wait_ge(res_done, n + 1)
                    dst = act_d[bass.ds(e, 1)].rearrange("o p t -> (o p) t")
                    sp.dma_start(dst, res[:, q % 2]).then_inc(res_out[q % 2], 16)
                if not last:
                    gates_out(4 * s + v)

            supersteps(sp, quarter)
            sp.wait_ge(lo_done, NQ + ETILES)
            for b in range(2):
                sp.dma_start(stage[:, (2 + b) * D:(3 + b) * D], v_cols[b]).then_inc(v_in[b], 16)
            for b in range(2):
                sp.wait_ge(res_out[b], 16 * ETILES // 2)
            for b in range(2):
                sp.dma_start(res[:, b], act_d[b]).then_inc(a_in[b], 16)
            sp.wait_ge(g_stored, 16 * (S // GBLK))

        @block.scalar
        def _(act):
            def queries(u):
                for b in range(2):
                    n = 2 * u + b
                    if not isint(n) or n > 0:
                        act.wait_ge(raw_in[1 - b], 16 * (u + 1 + b))
                        act.wait_ge(up_done, n)
                        nc.scalar.activation(c_hi[:, 1 - b], raw[:, 1 - b], ACT.Copy).then_inc(hi_done, 1)
                    act.wait_ge(up_done, n + 1)
                    act.wait_ge(sc_mm, 2 * u)
                    nc.scalar.activation(res[:, b], ps_up[:, b], ACT.Copy).then_inc(res_done, 1)
                for c in range(2):
                    act.wait_ge(sc_mm, 2 * u + c + 1)
                    act.wait_ge(sc_stored[c], 16 * u)
                    act.wait_ge(head_read, u)
                    nc.scalar.activation(sc_out[:, c], ps_s[:, c], ACT.Copy).then_inc(sc_copied, 1)

            queries(0)
            with loop(nc, act, 1, HEADS) as u:
                queries(u)

            def gates_hi(s, v, q):
                if q == 0:
                    act.wait_ge(g_stored, 16 * (4 * s + v))
                act.wait_ge(g_done, 16 * s + 4 * v + q + 1)
                nc.scalar.activation(g_buf[:, :, GT * q:GT * q + GT], ps_g[:, :, 0].rearrange("p t n -> p n t"),
                                     ACT.Copy).then_inc(g_half, 1)

            def quarter(s, v):
                first, last = (isint(v) and v == i for i in (0, 3))
                for q in range(4):
                    b = q % 2
                    e = 16 * s + 4 * v + q
                    n = e + NQ
                    k = 8 * s + 2 * v + q // 2
                    if not isint(n) or n + 1 <= last_n:
                        act.wait_ge(raw_in[1 - b], 16 * (k + NQ // 2 + 1 + b))
                        act.wait_ge(up_done, n)
                        nc.scalar.activation(c_hi[:, 1 - b], raw[:, 1 - b], ACT.Copy).then_inc(hi_done, 1)
                    if isint(v) and v == 0 and q == 0:
                        act.wait_ge(tile_routed, s + 1)
                        nc.scalar.activation(expd[:].rearrange("p h k -> p (h k)"), shifted[:], ACT.Exp).then_inc(exp_done, 1)
                    if first and q == 3:
                        gates_hi(s, v, 2)
                    elif last and q < 2:
                        gates_hi(s, v, 2 * q)
                    act.wait_ge(up_done, n + 1)
                    act.wait_ge(res_out[b], 16 * k)
                    nc.scalar.activation(res[:, b], ps_up[:, b], ACT.Gelu_apprx_tanh).then_inc(res_done, 1)
                    if last:
                        if q < 2:
                            gates_hi(s, v, 2 * q + 1)
                    elif not first or q == 3:
                        gates_hi(s, v, q)
                    elif q > 0:
                        gates_hi(s, v, q - 1)

            supersteps(act, quarter)

        @block.tensor
        def _(pe):
            def up(n, b, halfway=None, halves=(0, 1)):
                pe.wait_ge(hi_done, n + 1)
                pe.wait_ge(lo_done, n + 1)
                if not isint(n) or n >= 2:
                    pe.wait_ge(res_done, n - 1)
                for k in range(DC):
                    if halfway and k == DC // 2:
                        halfway()
                    for i, (w, h) in enumerate(((c_hi, h_hi), (c_hi, h_lo), (c_lo, h_hi))):
                        for half in halves:
                            mm = pe.matmul(ps_up[:, b, half], w[:, b, k], h[:, k, half * HALF:half * HALF + HALF],
                                           start=(k == 0 and i == 0), stop=(k == DC - 1 and i == 2))
                mm.then_inc(up_done, 1)

            def head(u, first):
                for b in range(2):
                    n = 2 * u + b
                    up(n, b, halves=(1,) if first else (0, 1))
                pe.wait_ge(keys_in, 16)
                for c in range(2):
                    pe.wait_ge(res_done, 2 * u + c + 1)
                    pe.wait_ge(sc_copied, 2 * u)
                    for t in range(TT):
                        mm = pe.matmul(ps_s[:, c, t], res[:, c, t * P:t * P + P], key_at(u, c), start=True, stop=True)
                    mm.then_inc(sc_mm, 1)

            def key_at(u, c):
                if isint(u):
                    return keys[:, 2 * u + c]
                return keys[:, bass.ds(2 * u + c, 1)].rearrange("p o n -> p (o n)")

            head(0, True)
            with loop(nc, pe, 1, HEADS) as u:
                head(u, False)
            pe.wait_ge(sc_copied, 2 * HEADS)

            def turn(s):
                pe.wait_ge(gates_done, s + 1)
                pe.wait_ge(g_copied, 16 * s)
                for i in range(3):
                    mm = pe.transpose(ps_s[:, 0, i], rt[:, i], ident[:])
                mm.then_inc(turned, 1)

            def gates(s, v, q):
                g = 16 * s + 4 * v + q
                pe.wait_ge(p_ready, 2 * g + 2)
                pe.wait_ge(q_ready, g + 1)
                pe.wait_ge(g_copied, g)
                for t in range(GT):
                    mm = pe.matmul(ps_g[:, t], first_hot[:, q % 2, t], second_gate[:, q % 2, t], start=True, stop=True)
                mm.then_inc(g_done, 1)

            def quarter(s, v):
                first, last = (isint(v) and v == i for i in (0, 3))
                for q in range(4):
                    between = 2 if first and q == 3 else 2 * q if last and q < 2 else None
                    up(16 * s + 4 * v + q + NQ, q % 2, None if between is None else lambda: gates(s, v, between))
                    if last:
                        if q < 2:
                            gates(s, v, 2 * q + 1)
                    elif not first:
                        gates(s, v, q)
                    elif q == 0:
                        turn(s)
                    else:
                        gates(s, v, (q - 1) if q < 3 else 3)

            supersteps(pe, quarter)

        @block.gpsimd
        def _(pool):
            nc.gpsimd.iota(iota_i[:], [[1, NKEY]], base=0, channel_multiplier=0).then_inc(consts, 1)
            pool.wait_ge(consts, 1)
            nc.gpsimd.tensor_copy(iota[:], iota_i[:]).then_inc(consts, 1)

            def quarter(s, v):
                for q in range(4):
                    g = 16 * s + 4 * v + q
                    pool.wait_ge(eq_ready, g + 1)
                    for i, part in enumerate((gate_hi, gate_lo)):
                        t0 = GT * 4 * v + GT * q
                        col = part[:, bass.ds(t0, GT)].bitcast(F32).unsqueeze(2).to_broadcast([P, GT, NKEY])
                        nc.gpsimd.tensor_tensor(second_gate[:, q % 2, :, i], second_hot[:, q % 2], col, ALU.mult).then_inc(p_ready, 1)

            supersteps(pool, quarter)

        @block.vector
        def _(dve):
            ch = Chain(dve, dve_step)

            def lo(n, b):
                dve.wait_ge(hi_done, n + 1)
                nc.vector.tensor_tensor(c_lo[:, b], raw[:, b], c_hi[:, b].bitcast(F32), ALU.subtract).then_inc(lo_done, 1)

            def route(sc, col):
                ch.sync()
                for r in range(2):
                    lo8 = slice(8 * r, 8 * r + 8)
                    src = [sc[c] if r == 0 else work[:, c] for c in range(2)]
                    for c in range(2):
                        if r == 1:
                            ch.sync(1)
                        ch.done(nc.vector.max(top[:, c, lo8], src[c]))
                    for c in range(2):
                        ch.sync(1)
                        ch.done(nc.vector.max_index(topi[:, c, lo8], top[:, c, lo8], src[c]))
                    if r == 0:
                        for c in range(2):
                            ch.done(nc.vector.match_replace(work[:, c], top[:, c, lo8], src[c], LOWEST))
                ch.sync()
                yield
                ch.done(nc.vector.tensor_copy(topf[:], topi[:]))
                ch.done(nc.vector.tensor_tensor(cand[:], top[:, 0].unsqueeze(2).to_broadcast([P, TOPK, TOPK]),
                                                top[:, 1].unsqueeze(1).to_broadcast([P, TOPK, TOPK]), ALU.add))
                flat = cand[:].rearrange("p a b -> p (a b)")
                flat2 = cand2[:].rearrange("p a b -> p (a b)")
                ch.sync()
                ch.done(nc.vector.max(best[:, 0:8], flat))
                ch.sync()
                ch.done(nc.vector.max_index(pos[:, 0:8], best[:, 0:8], flat))
                ch.done(nc.vector.match_replace(flat2, best[:, 0:8], flat, LOWEST))
                ch.sync()
                ch.done(nc.vector.max(best[:, 8:16], flat2))
                ch.sync()
                ch.done(nc.vector.max_index(pos[:, 8:16], best[:, 8:16], flat2))
                ch.done(nc.vector.tensor_scalar(shifted[:, bass.ds(col, TOPK)], best[:], best[:, 0:1], None, ALU.subtract))
                ch.sync()
                ch.done(nc.vector.tensor_scalar(pos2[:, 0], pos[:], 4, None, ALU.logical_shift_right))
                ch.done(nc.vector.tensor_scalar(pos2[:, 1], pos[:], 15, None, ALU.bitwise_and))
                ch.sync()
                ch.done(nc.vector.tensor_tensor(
                    pick[:], pos2[:].unsqueeze(3).to_broadcast([P, 2, TOPK, TOPK]),
                    iota[:, 0:TOPK].unsqueeze(1).unsqueeze(1).to_broadcast([P, 2, TOPK, TOPK]), ALU.is_equal))
                ch.sync()
                ch.done(nc.vector.tensor_tensor(pick2[:], pick[:],
                                                topf[:].unsqueeze(2).to_broadcast([P, 2, TOPK, TOPK]), ALU.mult))
                ch.sync()
                ch.done(nc.vector.tensor_reduce(idx[:, :, bass.ds(col, TOPK)], pick2[:], AX.X, ALU.add))
                ch.sync()

            dve.wait_ge(consts, 2)
            def head_routed(u):
                if not isint(u):
                    lo(2 * u + 1, 1)
                lo(2 * u + 2, 0)
                dve.wait_ge(sc_copied, 2 * u + 2)
                dve.nop(nofuse=True)
                for _ in route([sc_out[:, c, 0] for c in range(2)], u * TOPK):
                    dve.sem_inc(head_read, 1)
                ch.reset()

            head_routed(0)
            with loop(nc, dve, 1, HEADS) as u:
                head_routed(u)
            dve.sem_inc(tile_routed, 1)

            def finish_gates(s):
                dve.wait_ge(exp_done, s + 1)
                ch.done(nc.vector.tensor_reduce(esum[:], expd[:], AX.X, ALU.add))
                ch.sync()
                ch.done(nc.vector.reciprocal(einv[:], esum[:]))
                dve.wait_ge(turned, s)
                ch.done(nc.vector.tensor_copy(rt[:, 0:2], idx[:]))
                ch.sync()
                ch.done(nc.vector.tensor_tensor(rt[:, 2].rearrange("p (h k) -> p h k", h=HEADS), expd[:],
                                                einv[:].unsqueeze(2).to_broadcast([P, HEADS, TOPK]), ALU.mult))
                ch.sync()
                dve.sem_inc(gates_done, 1)

            def copy_turned(s):
                dve.wait_ge(turned, s + 1)
                dve.wait_ge(p_ready, 32 * s)
                ch.done(nc.vector.tensor_copy(idx_t[:], ps_s[:, 0, 0:2]))
                ch.done(nc.vector.tensor_copy(gate_hi[:], ps_s[:, 0, 2]))
                ch.sync()
                ch.done(nc.vector.tensor_tensor(gate_lo[:], ps_s[:, 0, 2], gate_hi[:].bitcast(F32), ALU.subtract))
                ch.sync()
                dve.sem_inc(turn_copied, 1)

            def onehots(s, v, q):
                g = 16 * s + 4 * v + q
                b = q % 2
                if not (isint(v) and v == 0 and q < 2):
                    dve.wait_ge(g_done, g - 1)
                    dve.wait_ge(p_ready, 2 * g - 2)
                else:
                    dve.wait_ge(g_done, 16 * s)
                t0 = GT * 4 * v + GT * q
                keyrow = iota[:].unsqueeze(1).to_broadcast([P, GT, NKEY])
                for i, out in ((1, second_hot), (0, first_hot)):
                    col = idx_t[:, i, bass.ds(t0, GT)].unsqueeze(2).to_broadcast([P, GT, NKEY])
                    nc.vector.tensor_tensor(out[:, b], keyrow, col, ALU.is_equal).then_inc((q_ready, eq_ready)[i], 1)

            def gates_lo(g, q):
                dve.wait_ge(g_half, g + 1)
                out = g_buf[:, :, GT * q:GT * q + GT]
                nc.vector.tensor_tensor(out, ps_g[:, :, 1].rearrange("p t n -> p n t"), out, ALU.add).then_inc(g_copied, 1)

            def final_quarter(s, v):
                g = 16 * s + 4 * v
                n = g + NQ
                onehots(s, v, 0)
                gates_lo(g - 1, 3)
                lo(n + 1, 1)
                onehots(s, v, 1)
                gates_lo(g, 0)
                onehots(s, v, 2)
                gates_lo(g + 1, 1)
                lo(n + 2, 0)
                onehots(s, v, 3)
                gates_lo(g + 2, 2)
                gates_lo(g + 3, 3)
                lo(n + 3, 1)
                ch.reset()

            def quarter(s, v):
                first = isint(v) and v == 0
                tail = isint(s) and s == TT - 1
                if isint(v) and v == 3:
                    final_quarter(s, v)
                    return
                for q in range(4):
                    g = 16 * s + 4 * v + q
                    n = g + NQ
                    if first and q == 1:
                        copy_turned(s)
                        onehots(s, v, 0)
                    elif q == 2 or not first and q == 0:
                        onehots(s, v, q)
                    if not first:
                        gates_lo(g - 1, (q - 1) % 4)
                    elif q > 1:
                        gates_lo(g - 2, q - 2)
                    if not isint(n) or n + 1 <= last_n:
                        lo(n + 1, 1 - q % 2)
                    if first and q == 0:
                        finish_gates(s)
                    elif first and q % 2:
                        onehots(s, v, q)
                    elif not first and q % 2 == 0:
                        onehots(s, v, q + 1)
                    if q % 2 == 0 and not tail:
                        dve.wait_ge(sc_loaded[q // 2], 16 * (4 * s + v + 1))
                        dve.nop(nofuse=True)
                        head = route([sc_in[:, q // 2, c] for c in range(2)], (2 * v + q // 2) * TOPK)
                        next(head)
                        dve.sem_inc(head_read, 1)
                    if not tail and q % 2 == first:
                        next(head, None)
                    if first and q == 3:
                        gates_lo(g - 1, 2)
                ch.reset()

            def token_tile(s):
                quarter(s, 0)
                with loop(nc, dve, 1, 4) as v:
                    quarter(s, v)
                dve.sem_inc(tile_routed, 1)
                gates_lo(16 * s + 15, 3)

            token_tile(0)
            with loop(nc, dve, 1, TT - 1) as s:
                token_tile(s)
            quarter(TT - 1, 0)
            with loop(nc, dve, 1, 3) as v:
                quarter(TT - 1, v)
            quarter(TT - 1, 3)


GROUP = 4
NGROUP = ETILES // GROUP


def down_and_finish(nc, stage, act_d, gate_d, v_cols, v_in, a_in, x_mid, gain, out):
    with ExitStack() as ctx:
        sb = lambda n, s, d=F32: ctx.enter_context(nc.sbuf_tensor(n, s, d))
        sem = lambda n: ctx.enter_context(nc.semaphore(n))
        a_raw = stage[:, 0:2 * S].rearrange("p (b t) -> p b t", b=2)
        v_raw = stage[:, 2 * D:4 * D].rearrange("p (b n) -> p b n", b=2)
        g_raw = sb("g_raw", [P, S // GBLK, GROUP, GBLK])
        v_hi = sb("v_hi", [P, 2, GROUP, D], F32R)
        v_lo = sb("v_lo", [P, 2, GROUP, D], F32R)
        c_hi = sb("coef_hi", [P, 2, GROUP, S], F32R)
        c_lo = sb("coef_lo", [P, 2, GROUP, S], F32R)
        acc = sb("acc", [P, TT, D])
        gained = sb("y_gained", [P, 2, D])
        ss = sb("y_ss", [P, TT])
        rs = sb("y_rs", [P, TT])
        rr = sb("y_rr", [P, TT])
        eps = sb("y_eps", [P, 1])
        ps = ctx.enter_context(nc.psum_tensor("ps_y", [P, 4, 2, HALF], F32))

        g_in = sem("g_in")
        coef, coef_hi, coef_lo = sem("coef"), sem("coef_hi_done"), sem("coef_lo_done")
        vhi_done, vlo_done = sem("vhi_done"), sem("vlo_done")
        y_mm, y_added = sem("y_mm"), sem("y_added")
        eps_ready = sem("y_eps_ready")
        x_in = [sem("x_in0"), sem("x_in1")]
        sq_done, root_done, inv_done, out_ready = sem("sq_done"), sem("root_done"), sem("inv_done"), sem("out_ready")
        stored = sem("stored")
        dve_step = sem("dve_step_b")
        block = ctx.enter_context(nc.Block())

        @block.sync
        def _(sp):
            def gates_in(m):
                if not isinstance(m, int) or m > 0:
                    sp.wait_ge(coef, GROUP * m)
                src = gate_d[:, :, bass.ds(GROUP * m, GROUP), :].rearrange("b p j t -> p b (j t)")
                sp.dma_start(g_raw[:].rearrange("p b j t -> p b (j t)"), src).then_inc(g_in, 16)

            def load(m, j):
                e = GROUP * m + j
                b = j % 2
                if isinstance(m, int) and m == 0 and j < 2:
                    return
                sp.wait_ge(coef_lo, e - 1)
                sp.dma_start(a_raw[:, b], act_d[bass.ds(e, 1)].rearrange("o p t -> (o p) t")).then_inc(a_in[b], 16)
                sp.wait_ge(vlo_done, e - 1)
                sp.dma_start(v_raw[:, b], v_cols[bass.ds(e, 1)].rearrange("o p d -> (o p) d")).then_inc(v_in[b], 16)

            gates_in(0)
            for j in range(GROUP):
                load(0, j)
            with loop(nc, sp, 1, NGROUP) as m:
                gates_in(m)
                for j in range(GROUP):
                    load(m, j)
            sp.wait_ge(y_mm, TT * (NGROUP - 1))
            for t in range(TT):
                if t >= 2:
                    sp.wait_ge(out_ready, t - 1)
                else:
                    sp.wait_ge(coef_lo, ETILES)
                sp.dma_start(a_raw[:, t % 2], x_mid[t * P:t * P + P]).then_inc(x_in[t % 2], 16)
                if t >= 1:
                    sp.wait_ge(out_ready, t)
                    sp.dma_start(out[(t - 1) * P:t * P], acc[:, t - 1]).then_inc(stored, 16)
            sp.wait_ge(out_ready, TT)
            sp.dma_start(out[(TT - 1) * P:TT * P], acc[:, TT - 1]).then_inc(stored, 16)
            sp.wait_ge(stored, 16 * TT)

        @block.scalar
        def _(act):
            def split(m, p, j):
                b = j % 2
                act.wait_ge(v_in[b], 16 * (2 * m + j // 2 + 1))
                if not (isinstance(m, int) and m < 2):
                    act.wait_ge(y_mm, TT * (m - 1))
                nc.scalar.activation(v_hi[:, p, j], v_raw[:, b], ACT.Copy).then_inc(vhi_done, 1)
                act.wait_ge(coef, GROUP * m + j + 1)
                nc.scalar.activation(c_hi[:, p, j], a_raw[:, b], ACT.Copy).then_inc(coef_hi, 1)

            for m in range(2):
                for j in range(GROUP):
                    split(m, m, j)
            with loop(nc, act, 1, NGROUP // 2) as w:
                for p in range(2):
                    for j in range(GROUP):
                        split(2 * w + p, p, j)
            act.wait_ge(eps_ready, 1)
            for t in range(TT):
                act.wait_ge(y_added, TT * (NGROUP - 1) + t + 1)
                if t >= 2:
                    act.wait_ge(sq_done, t - 1)
                nc.scalar.activation(v_raw[:, t % 2], acc[:, t], ACT.Square, accum_out=ss[:, t:t + 1]).then_inc(sq_done, 1)
                act.wait_ge(sq_done, t + 1)
                nc.scalar.activation(rs[:, t:t + 1], ss[:, t:t + 1], ACT.Sqrt, bias=eps[:], scale=1.0 / D).then_inc(root_done, 1)

        @block.tensor
        def _(pe):
            def products(t, p, j):
                for i, (c, v) in enumerate(((c_hi, v_hi), (c_hi, v_lo), (c_lo, v_hi))):
                    for half in range(2):
                        mm = pe.matmul(ps[:, t % 4, half], c[:, p, j, t * P:t * P + P],
                                       v[:, p, j, half * HALF:half * HALF + HALF],
                                       start=(j == 0 and i == 0), stop=(j == GROUP - 1 and i == 2))
                return mm

            def group(m, p, first=0):
                for t in range(first, TT):
                    pe.wait_ge(coef_lo, GROUP * m + GROUP)
                    pe.wait_ge(vlo_done, GROUP * m + GROUP)
                    pe.wait_ge(y_added, TT * m + t - 3)
                    for j in range(GROUP):
                        mm = products(t, p, j)
                    mm.then_inc(y_mm, 1)

            for j in range(GROUP):
                pe.wait_ge(coef_lo, j + 1)
                pe.wait_ge(vlo_done, j + 1)
                for t in range(4):
                    mm = products(t, 0, j)
                    if j == GROUP - 1:
                        mm.then_inc(y_mm, 1)
            group(0, 0, first=4)
            group(1, 1)
            with loop(nc, pe, 1, NGROUP // 2) as w:
                group(2 * w, 0)
                group(2 * w + 1, 1)

        @block.vector
        def _(dve):
            nc.vector.memset(eps[:], EPS).then_inc(eps_ready, 1)

            def product(m, p, j):
                b = j % 2
                e = GROUP * m + j
                if j == 0:
                    dve.wait_ge(g_in, 16 * (m + 1))
                dve.wait_ge(a_in[b], 16 * (2 * m + j // 2 + 1))
                a = a_raw[:, b].rearrange("p (k t) -> p k t", t=GBLK)
                nc.vector.tensor_tensor(a, a, g_raw[:, :, j], ALU.mult).then_inc(coef, 1)
                dve.wait_ge(vhi_done, e + 1)
                nc.vector.tensor_tensor(v_lo[:, p, j], v_raw[:, b], v_hi[:, p, j].bitcast(F32), ALU.subtract).then_inc(vlo_done, 1)
                dve.wait_ge(coef_hi, e + 1)
                nc.vector.tensor_tensor(c_lo[:, p, j], a_raw[:, b], c_hi[:, p, j].bitcast(F32), ALU.subtract).then_inc(coef_lo, 1)

            def add(m, t):
                total = ps[:, t % 4].rearrange("p a b -> p (a b)")
                dve.wait_ge(y_mm, TT * m + t + 1)
                if isinstance(m, int) and m == 0:
                    nc.vector.tensor_copy(acc[:, t], total).then_inc(y_added, 1)
                    return
                dve.wait_ge(y_added, TT * m - TT + t + 1)
                nc.vector.tensor_tensor(acc[:, t], total, acc[:, t], ALU.add).then_inc(y_added, 1)

            def step(m, p):
                for j in range(GROUP):
                    product(m + 1, 1 - p, j)
                    add(m, 2 * j)
                    add(m, 2 * j + 1)

            for j in range(GROUP):
                product(0, 0, j)
            step(0, 0)
            with loop(nc, dve, 0, NGROUP // 2 - 1) as w:
                step(2 * w + 1, 1)
                step(2 * w + 2, 0)
            for t in range(TT):
                add(NGROUP - 1, t)
                dve.wait_ge(y_added, TT * (NGROUP - 1) + t + 1)
                if t >= 2:
                    dve.wait_ge(out_ready, t - 1)
                nc.vector.tensor_tensor(gained[:, t % 2], acc[:, t], gain[:], ALU.mult).then_inc(dve_step, 1)
                dve.wait_ge(root_done, t + 1)
                nc.vector.reciprocal(rr[:, t:t + 1], rs[:, t:t + 1]).then_inc(inv_done, 1)
                dve.wait_ge(inv_done, t + 1)
                dve.wait_ge(dve_step, t + 1)
                dve.wait_ge(x_in[t % 2], 16 * (t // 2 + 1))
                nc.vector.scalar_tensor_tensor(out=acc[:, t], in0=gained[:, t % 2], scalar=rr[:, t:t + 1], in1=a_raw[:, t % 2],
                                               op0=ALU.mult, op1=ALU.add).then_inc(out_ready, 1)



COLW = 256
HEADS_A = 4
DH = 64
VD = 128
NADA = 6
NW = 4
NL = 3
LAM_INIT = 0.8 - 0.6 * math.exp(-0.3 * 0)
RB = 32
RLEN = 3 * P - 1
SGU_G = 8
SW = 512


class Weights:

    def __init__(self, nc, ctx, w_in, stage):
        sb = lambda n, d=F32: ctx.enter_context(nc.sbuf_tensor(n, [P, 2, DC, COLW], d))
        sem = lambda n: ctx.enter_context(nc.semaphore(n))
        self.source = w_in
        self.raw = stage[:].rearrange("p (b k n) -> p b k n", b=2, k=DC)
        self.hi, self.lo = sb("wi_hi", F32R), sb("wi_lo", F32R)
        self.loaded = [sem("wi_in0"), sem("wi_in1")]
        self.hi_done, self.lo_done = sem("wi_hi_done"), sem("wi_lo_done")

    def load(self, sp, g):
        if g >= 2:
            sp.wait_ge(self.lo_done, g - 1)
        sp.dma_start(self.raw[:, g % 2], self.source[g]).then_inc(self.loaded[g % 2], 16)

    def split_hi(self, nc, act, g):
        act.wait_ge(self.loaded[g % 2], 16 * (g // 2 + 1))
        nc.scalar.activation(self.hi[:, g % 2], self.raw[:, g % 2], ACT.Copy).then_inc(self.hi_done, 1)

    def split_lo(self, nc, dve, g):
        dve.wait_ge(self.hi_done, g + 1)
        nc.vector.tensor_tensor(self.lo[:, g % 2], self.raw[:, g % 2], self.hi[:, g % 2].bitcast(F32), ALU.subtract).then_inc(self.lo_done, 1)


class Columns:

    def __init__(self, nc, ctx, stage):
        sem = lambda n: ctx.enter_context(nc.semaphore(n))
        self.raw = stage[:, 2 * D:4 * D].rearrange("p (b k n) -> p b k n", b=2, k=DC)
        self.hi, self.lo = (ctx.enter_context(nc.sbuf_tensor(n, [P, 2, DC, P], F32R)) for n in ("col_hi", "col_lo"))
        self.loaded = [sem("col_in0"), sem("col_in1")]
        self.hi_done, self.lo_done = sem("col_hi_done"), sem("col_lo_done")
        self.ps = ctx.enter_context(nc.psum_tensor("ps_up", [P, 2, 2, HALF], F32))


def modulate_and_norm(nc, x, c_col, w_ada, b_ada, g_col, ident, ones, c_silu, x_t, mod_cols, gain1, gain2, w, z_t, z_n):
    with ExitStack() as ctx:
        sb = lambda n, s, d=F32: ctx.enter_context(nc.sbuf_tensor(n, s, d))
        sems = []

        def sem(n):
            sems.append(ctx.enter_context(nc.semaphore("f1_" + n)))
            return sems[-1]

        wbuf, xs = z_t[:, 0:NW], z_n
        modb = (gain1, gain2)
        squares = w.raw[:, 0, 0:D // COLW].rearrange("p k n -> p (k n)")
        bias = w.raw[:, 1].rearrange("p (i k) n -> p i (k n)", i=2)
        c_wide = sb("c_silu_wide", [P, DC, P])
        gcol = sb("g_col_s", [P, 4, DC])
        craw = sb("c_raw", [P, DC])
        ssq = sb("ssq", [P, TT])
        root = sb("x_root", [P, TT])
        inv = sb("x_inv", [P, TT])
        eps = sb("eps_f1", [P, 1])
        ps_m = ctx.enter_context(nc.psum_tensor("ps_m", [P, 2, HALF], F32))
        ps_c = ctx.enter_context(nc.psum_tensor("ps_c", [P, DC, P], F32))
        ps_x = ctx.enter_context(nc.psum_tensor("ps_x", [P, 2, DC, P], F32))
        c_in, g_in, b_in = sem("c_in"), sem("g_in"), sem("b_in")
        w_ld = [sem(f"w_in{i}") for i in range(NW)]
        x_ld = [sem(f"x_in{i}") for i in range(TT)]
        ready, silu_done, wide_done, ident_done = sem("ready"), sem("silu"), sem("wide"), sem("ident")
        chunk_used, mod_mm, mod_done, cols_mm, cols_done = map(sem, "chunk_used mod_mm mod_done cols_mm cols_done".split())
        sq_done, rt_done, inv_done, scaled, x_turned, x_copied = map(sem, "sq rt inv scaled turned copied".split())
        block = ctx.enter_context(nc.Block())

        @block.sync
        def _(sp):
            sp.dma_start(craw[:], c_col).then_inc(c_in, 16)
            for n in range(2 * DC):
                if n >= NW:
                    sp.wait_ge(chunk_used, n - NW + 1)
                sp.dma_start(wbuf[:, n % NW], w_ada[n // DC, n % DC]).then_inc(w_ld[n % NW], 16)
                if n == NW:
                    sp.dma_start(bias.rearrange("p a b -> p (a b)"), b_ada[0:1, 0:2 * D].to_broadcast([P, 2 * D])).then_inc(b_in, 16)
                    sp.dma_start(gcol[:], g_col).then_inc(g_in, 16)
            sp.wait_ge(sq_done, TT)
            w.load(sp, 0)

        @block.scalar
        def _(act):
            for t in range(TT):
                act.dma_start(xs[:, t], x[t * P:t * P + P]).then_inc(x_ld[t], 16)
            act.wait_ge(c_in, 16)
            nc.scalar.activation(c_silu[:], craw[:], ACT.Silu).then_inc(silu_done, 1)
            act.wait_ge(ready, 2)

            def copy_turned(t):
                act.wait_ge(x_turned, t + 1)
                nc.scalar.activation(x_t[:, :, t * P:t * P + P], ps_x[:, t % 2], ACT.Copy).then_inc(x_copied, 1)

            for t in range(TT):
                act.wait_ge(x_ld[t], 16)
                if t >= 1:
                    act.wait_ge(sq_done, t)
                nc.scalar.activation(squares, xs[:, t], ACT.Square, accum_out=ssq[:, t:t + 1]).then_inc(sq_done, 1)
                act.wait_ge(sq_done, t + 1)
                nc.scalar.activation(root[:, t:t + 1], ssq[:, t:t + 1], ACT.Sqrt, bias=eps[:], scale=1.0 / D).then_inc(rt_done, 1)
                if t >= 2:
                    copy_turned(t - 2)
            copy_turned(TT - 2)
            copy_turned(TT - 1)
            w.split_hi(nc, act, 0)

        @block.gpsimd
        def _(pool):
            nc.gpsimd.memset(ident[:], 0.0).then_inc(ident_done, 1)
            pool.wait_ge(ident_done, 1)
            nc.gpsimd.affine_select(out=ident[:], in_=ident[:], compare_op=ALU.not_equal, fill=1.0, base=0,
                                    pattern=[[-1, P]], channel_multiplier=1).then_inc(ident_done, 1)

        @block.tensor
        def _(pe):
            pe.wait_ge(wide_done, 1)
            pe.wait_ge(ident_done, 2)

            def columns(i):
                pe.wait_ge(mod_done, i + 1)
                if i:
                    pe.wait_ge(cols_done, i)
                for k in range(DC):
                    mm = pe.transpose(ps_c[:, k], modb[i][:, k * P:k * P + P], ident[:])
                mm.then_inc(cols_mm, 1)

            for n in range(2 * DC):
                i, k = n // DC, n % DC
                pe.wait_ge(w_ld[n % NW], 16 * (n // NW + 1))
                if i == 1 and k == 0:
                    pe.wait_ge(mod_done, 1)
                for half in range(2):
                    mm = pe.matmul(ps_m[:, half], c_wide[:, k], wbuf[:, n % NW, half * HALF:half * HALF + HALF],
                                   start=(k == 0), stop=(k == DC - 1))
                mm.then_inc(chunk_used, 1)
                if n % 2:
                    t = n // 2
                    pe.wait_ge(scaled, t + 1)
                    if t >= 2:
                        pe.wait_ge(x_copied, t - 1)
                    for c in range(DC):
                        mm = pe.transpose(ps_x[:, t % 2, c], xs[:, t, c * P:c * P + P], ident[:])
                    mm.then_inc(x_turned, 1)
                if n == 11:
                    columns(0)
            columns(1)

        @block.vector
        def _(dve):
            nc.vector.memset(ones[:], 1.0).then_inc(ready, 1)
            nc.vector.memset(eps[:], EPS).then_inc(ready, 1)
            dve.wait_ge(silu_done, 1)
            nc.vector.tensor_copy(c_wide[:], c_silu[:].unsqueeze(2).to_broadcast([P, DC, P])).then_inc(wide_done, 1)

            def scale_rows(t):
                dve.wait_ge(rt_done, t + 1)
                nc.vector.reciprocal(inv[:, t:t + 1], root[:, t:t + 1]).then_inc(inv_done, 1)
                dve.wait_ge(inv_done, t + 1)
                nc.vector.tensor_scalar(xs[:, t], xs[:, t], inv[:, t:t + 1], None, ALU.mult).then_inc(scaled, 1)

            for i in range(2):
                for t in range(TT // 2 * i, TT // 2 * (i + 1)):
                    scale_rows(t)
                    if t == TT - 2:
                        dve.wait_ge(cols_mm, 1)
                        nc.vector.tensor_copy(mod_cols[:, 1], ps_c[:, :, 0]).then_inc(cols_done, 1)
                dve.wait_ge(chunk_used, DC * (i + 1))
                dve.wait_ge(b_in, 16)
                nc.vector.tensor_tensor(modb[i][:], ps_m[:].rearrange("p a b -> p (a b)"), bias[:, i], ALU.add).then_inc(mod_done, 1)
            dve.wait_ge(cols_mm, 2)
            dve.wait_ge(g_in, 16)
            nc.vector.scalar_tensor_tensor(out=mod_cols[:, 0], in0=ps_c[:, :, 0], scalar=1.0, in1=gcol[:, 0],
                                           op0=ALU.add, op1=ALU.mult).then_inc(cols_done, 1)
            w.split_lo(nc, dve, 0)

    return sems


def affine_cols(nc, dve, out, src, scale, shift, step, before):
    nc.vector.tensor_tensor(out, src, scale.unsqueeze(2).to_broadcast([P, DC, P]), ALU.mult).then_inc(step, 1)
    dve.wait_ge(step, before + 1)
    nc.vector.tensor_tensor(out, out, shift.unsqueeze(2).to_broadcast([P, DC, P]), ALU.add).then_inc(step, 1)


def in_project(nc, w, w_ada, b_ada, norm_g, g_col, ident, ones, c_silu, x_t, mod_cols, gain1, gain2, h_hi, h_lo, z_t, z_n, sgu_ln, spent):
    with ExitStack() as ctx:
        sb = lambda n, s, d=F32: ctx.enter_context(nc.sbuf_tensor(n, s, d))
        sem = lambda n: ctx.enter_context(nc.semaphore("f2_" + n))
        NG = 10
        ROWS = 4
        gcol = sb("g_col_s2", [P, 4, DC])
        ln_rows = sb("ln_rows", [P, 2, SW])
        stats = sb("ln_stats", [P, TT, 6])
        mv = sb("ln_mv", [P, TT, 2])
        lnr = sb("ln_root", [P, TT])
        lni = sb("ln_inv", [P, TT])
        eps = sb("eps_f3", [P, 1])
        ps = ctx.enter_context(nc.psum_tensor("ps_z", [P, 2, 2, HALF], F32))
        ps_m = ctx.enter_context(nc.psum_tensor("ps_m2", [P, 2, HALF], F32))
        ps_c = ctx.enter_context(nc.psum_tensor("ps_c2", [P, DC, P], F32))
        chunk = [z_n[:, i] for i in range(NW)]
        part = [z_n[:, NW], z_n[:, NW + 1]]
        bias_at = [z_n[:, NW + 2]] * 3 + [z_n[:, NW + 3]]
        norm_gain = z_n[:, NW + 3]
        used, mm_done, copied = sem("used"), sem("mm"), sem("copied")
        h_full, h_hid, h_lod = sem("h_full"), sem("h_hi"), sem("h_lo")
        w_ld = [sem(f"ada_in{i}") for i in range(NW)]
        bias_in, gain_in, gcol_in = sem("bias_in"), sem("gain_in"), sem("gcol_in")
        ln_ld, stat_done, agg, root, ln_step, eps_ready = map(sem, "ln_ld stat agg root ln_step eps".split())
        sliced, mod_mm, summed, mod_done, cols_mm, cols_done = map(sem, "sliced mod_mm summed mod_done cols_mm cols_done".split())
        block = ctx.enter_context(nc.Block())

        @block.sync
        def _(sp):
            def ada(r, chunks):
                for k in chunks:
                    n = DC * r + k
                    if n >= NW:
                        sp.wait_ge(sliced, n - NW + 1)
                    sp.dma_start(chunk[n % NW], w_ada[2 + r, k]).then_inc(w_ld[n % NW], 16)

            def rows(r):
                if r in (1, 2):
                    sp.wait_ge(mod_done, r + 1)
                sp.dma_start(bias_at[r], b_ada[0:1, (2 + r) * D:(3 + r) * D].to_broadcast([P, D])).then_inc(bias_in, 16)
                if r < 2:
                    sp.dma_start(norm_gain, norm_g[2 * r + 1:2 * r + 2, :].to_broadcast([P, D])).then_inc(gain_in, 16)

            first, second = range(NW), range(NW, DC)
            w.load(sp, 1)
            sp.dma_start(gcol[:], g_col).then_inc(gcol_in, 16)
            ada(0, first)
            rows(0)
            w.load(sp, 2)
            ada(0, second)
            w.load(sp, 3)
            ada(1, first)
            w.load(sp, 4)
            ada(1, second)
            ada(2, first)
            w.load(sp, 5)
            rows(1)
            ada(2, second)
            ada(3, first)
            w.load(sp, 6)
            rows(2)
            rows(3)
            ada(3, second)
            for i in range(2):
                sp.dma_start(ln_rows[:, i], sgu_ln[i:i + 1].to_broadcast([P, SW])).then_inc(ln_ld, 16)
            for g in range(7, NG):
                w.load(sp, g)

        @block.scalar
        def _(act):
            for k in range(DC):
                act.wait_ge(h_full, k + 1)
                nc.scalar.activation(h_hi[:, k], x_t[:, k], ACT.Copy).then_inc(h_hid, 1)
            w.split_hi(nc, act, 1)
            for g in range(NG):
                for j in range(2 if g < 6 else 4):
                    m = 2 * g + j if g < 6 else 12 + 4 * (g - 6) + j
                    act.wait_ge(mm_done, m + 1)
                    if g < 6:
                        func = ACT.Gelu_apprx_tanh if m < 4 else ACT.Copy
                        nc.scalar.activation(z_t[:, m], ps[:, j], func).then_inc(copied, 1)
                    else:
                        act.wait_ge(cols_mm, 2)
                        nc.scalar.activation(z_n[:, 2 * j:2 * j + 2, COLW * (g - 6):COLW * (g - 5)], ps[:, j % 2, :, 0:COLW],
                                             ACT.Gelu_apprx_tanh if g < 8 else ACT.Copy).then_inc(copied, 1)
                if g + 2 < NG:
                    act.wait_ge(used, g + 1)
                    w.split_hi(nc, act, g + 2)
                if g == 8:
                    act.wait_ge(agg, TT)
                    act.wait_ge(eps_ready, 1)
                    nc.scalar.activation(lnr[:], mv[:, :, 1], ACT.Sqrt, bias=eps[:]).then_inc(root, 1)

        @block.gpsimd
        def _(pool):
            for s in spent:
                pool.sem_clear(s)

        @block.tensor
        def _(pe):
            passes = ((w.hi, h_hi), (w.hi, h_lo), (w.lo, h_hi))

            def features(v, b):
                pe.wait_ge(w.lo_done, 2 * v + b + 1)
                for j in range(2):
                    m = 4 * v + 2 * b + j
                    first = isinstance(v, int) and b == 0
                    if not first:
                        pe.wait_ge(copied, m - 1)
                    for k in range(DC):
                        if first and j == 0:
                            pe.wait_ge(h_lod, k + 1)
                        for i, (a, h) in enumerate(passes):
                            for half in range(2):
                                mm = pe.matmul(ps[:, j, half], a[:, b, k, j * P:j * P + P], h[:, k, half * HALF:half * HALF + HALF],
                                               start=(k == 0 and i == 0), stop=(k == DC - 1 and i == 2))
                    mm.then_inc(mm_done, 1)
                pe.wait_ge(mm_done, 4 * v + 2 * b + 2)
                pe.sem_inc(used, 1)

            def tokens(v, b):
                pe.wait_ge(w.lo_done, 2 * v + b + 7)
                for j in range(4):
                    m = 8 * v + 4 * b + j + 12
                    pe.wait_ge(copied, m - 1)
                    for a in range(2):
                        t = 2 * j + a
                        for k in range(DC):
                            for i, (wt, h) in enumerate(((w.hi, h_hi), (w.hi, h_lo), (w.lo, h_hi))):
                                mm = pe.matmul(ps[:, j % 2, a, 0:COLW], h[:, k, t * P:t * P + P], wt[:, b, k],
                                               start=(k == 0 and i == 0), stop=(k == DC - 1 and i == 2))
                    mm.then_inc(mm_done, 1)
                pe.wait_ge(mm_done, 8 * v + 4 * b + 16)
                pe.sem_inc(used, 1)

            def total(r, b):
                pe.wait_ge(sliced, DC * r + DC)
                pe.wait_ge(mod_done, r + 1)
                for half in range(2):
                    mm = pe.matmul(ps_m[:, half], ones[:], part[b][:, half * HALF:half * HALF + HALF], start=True, stop=True)
                mm.then_inc(mod_mm, 1)

            features(0, 0)
            features(0, 1)
            with loop(nc, pe, 1, 3) as v:
                for b in range(2):
                    total(2 * v + b - 2, b)
                    features(v, b)
            for n in range(2):
                pe.wait_ge(mod_done, 4 + n)
                if n:
                    pe.wait_ge(cols_done, n)
                for k in range(DC):
                    mm = pe.transpose(ps_c[:, k], bias_at[2 + n][:, k * P:k * P + P], ident[:])
                mm.then_inc(cols_mm, 1)
            with loop(nc, pe, 0, 2) as v:
                tokens(v, 0)
                tokens(v, 1)

        @block.vector
        def _(dve):
            dve.sem_inc(mod_done, 1)

            def h_lo_part(k):
                dve.wait_ge(h_hid, k + 1)
                nc.vector.tensor_tensor(h_lo[:, k], x_t[:, k], h_hi[:, k].bitcast(F32), ALU.subtract).then_inc(h_lod, 1)

            for k in range(DC):
                nc.vector.tensor_scalar(x_t[:, k], x_t[:, k], mod_cols[:, 0, k:k + 1], mod_cols[:, 1, k:k + 1],
                                        ALU.mult, ALU.add).then_inc(h_full, 1)
                if k:
                    h_lo_part(k - 1)
            h_lo_part(DC - 1)
            w.split_lo(nc, dve, 1)

            def row(r):
                dst = part[r % 2]
                for k in range(DC):
                    n = DC * r + k
                    dve.wait_ge(w_ld[n % NW], 16 * (n // NW + 1))
                    if k == 0:
                        if r >= 2:
                            dve.wait_ge(mod_mm, r - 1)
                        nc.vector.tensor_scalar(dst, chunk[n % NW], c_silu[:, 0:1], None, ALU.mult).then_inc(sliced, 1)
                    else:
                        dve.wait_ge(sliced, n)
                        nc.vector.scalar_tensor_tensor(out=dst, in0=chunk[n % NW], scalar=c_silu[:, k:k + 1], in1=dst,
                                                       op0=ALU.mult, op1=ALU.add).then_inc(sliced, 1)

            def finish(r):
                dve.wait_ge(mod_mm, r + 1)
                dve.wait_ge(bias_in, 16 * (r + 1) if r < 2 else 16 * ROWS)
                gain = (gain1, gain2)[r][:] if r < 2 else bias_at[r]
                nc.vector.tensor_tensor(gain, ps_m[:].rearrange("p a b -> p (a b)"), bias_at[r], ALU.add).then_inc(summed, 1)
                if r < 2:
                    dve.wait_ge(summed, r + 1)
                    dve.wait_ge(gain_in, 16 * (r + 1))
                    nc.vector.tensor_tensor(gain, gain, norm_gain, ALU.mult).then_inc(mod_done, 1)
                else:
                    dve.wait_ge(summed, r + 1)
                    dve.sem_inc(mod_done, 1)

            row(0)
            for r in range(1, ROWS + 3):
                w.split_lo(nc, dve, r + 1)
                if 2 <= r < ROWS + 2:
                    finish(r - 2)
                if r < ROWS:
                    row(r)
            dve.wait_ge(cols_mm, 1)
            nc.vector.tensor_copy(mod_cols[:, 3], ps_c[:, :, 0]).then_inc(cols_done, 1)
            dve.wait_ge(cols_mm, 2)
            dve.wait_ge(gcol_in, 16)
            nc.vector.scalar_tensor_tensor(out=mod_cols[:, 2], in0=ps_c[:, :, 0], scalar=1.0, in1=gcol[:, 2],
                                           op0=ALU.add, op1=ALU.mult).then_inc(cols_done, 1)
            w.split_lo(nc, dve, 8)
            w.split_lo(nc, dve, 9)
            ch = Chain(dve, ln_step)
            nc.vector.memset(eps[:], EPS).then_inc(eps_ready, 1)
            for t in range(TT):
                dve.wait_ge(copied, 12 + 4 + t // 2 + 1)
                nc.vector.bn_stats(stats[:, t], z_n[:, t, 0:SW]).then_inc(stat_done, 1)
            for t in range(TT):
                dve.wait_ge(stat_done, t + 1)
                nc.vector.bn_aggr(mv[:, t], stats[:, t]).then_inc(agg, 1)
            dve.wait_ge(root, 1)
            ch.done(nc.vector.reciprocal(lni[:], lnr[:]))
            ch.sync()
            for t in range(TT):
                ch.done(nc.vector.tensor_scalar(z_n[:, t, 0:SW], z_n[:, t, 0:SW], mv[:, t, 0:1], lni[:, t:t + 1],
                                                ALU.subtract, ALU.mult))
            ch.sync()
            dve.wait_ge(ln_ld, 32)
            v = z_n[:, :, 0:SW]
            for i, op in enumerate((ALU.mult, ALU.add)):
                ch.done(nc.vector.tensor_tensor(v, v, ln_rows[:, i].unsqueeze(1).to_broadcast([P, TT, SW]), op))
                ch.sync()


def mix(nc, z_t, z_n, stage, sgu_wt, sgu_b, lam_p, subln_col, rel_bias, bucket_hot, tbl_d, ident, cat_hi, cat_lo, w_out, wo_ld):
    with ExitStack() as ctx:
        sb = lambda n, s, d=F32: ctx.enter_context(nc.sbuf_tensor(n, s, d))
        sem = lambda n: ctx.enter_context(nc.semaphore("mx_" + n))
        bt = sb("sgu_bias", [P, SGU_G // 2, P])
        eps = sb("eps_f4", [P, 1])
        rb = sb("rel_b", [RB, HEADS_A])
        rbb = sb("rel_bb", [RB, HEADS_A, P])
        hot = sb("hot", [RB, RLEN])
        far = sb("far_bias", [P, HEADS_A])
        far_pair = sb("far_pair", [P, 2])
        tb = sb("near_bias", [P, HEADS_A, 2 * P])
        lam = sb("lam_s", [P, 4, DH])
        lamw = sb("lam_w", [P, 2, DH])
        lamd = sb("lam_d", [P, 2])
        lame = sb("lam_e", [P, 2])
        neglam = sb("neg_lam", [P, 1])
        sg = sb("subln_in", [P, 1])
        sgs = sb("subln_scaled", [P, 1])
        logit = sb("logit", [P, NL, 2, S])
        att = stage[:, 0:2 * S].rearrange("p (b s) -> p b s", b=2)
        att_t = stage[:, 2 * S:4 * S].rearrange("p (b k s) -> p b k s", b=2, k=TT)
        wt = logit[:, 2, 0].rearrange("p (g t) -> p g t", g=SGU_G)
        nmax = sb("nmax", [P, 2, 2])
        mx = sb("mx", [P, 2, 2])
        ssum = sb("ssum", [P, 2, 2])
        sinv = sb("sinv", [P, 2, 2])
        fac = sb("fac", [P, 2])
        sq_row = sb("o_squares", [P, VD])
        osq = sb("osq", [P, TT, HEADS_A])
        ort = sb("ort", [P, TT, HEADS_A])
        oin = sb("oin", [P, TT, HEADS_A])
        ps_l = ctx.enter_context(nc.psum_tensor("ps_l", [P, 4, HALF], F32))
        ps_t = ctx.enter_context(nc.psum_tensor("ps_t", [P, TT, P], F32))
        ps_o = ctx.enter_context(nc.psum_tensor("ps_o", [P, 2, HALF], F32))
        o_all = z_n[:, :, 0:SW]
        pair_qk = z_t[:, 0:4]
        logit_row = logit[:].rearrange("p a b s -> p (a b s)")
        ps_row = ps_l[:].rearrange("p c s -> p (c s)")
        ps_far = ps_row[:, 0:3 * HALF].rearrange("p (c s) -> p c s", c=2)
        ps_near = ps_l[:, 3].rearrange("p (c s) -> p c s", c=2)

        w_ld, bt_ld, small_ld, tb_st, tb_ld = map(sem, "w_ld bt_ld small_ld tb_st tb_ld".split())
        masked, tb_masked, ready, tb_mm, tb_copied, lam_exp = map(sem, "masked tb_masked ready tb_mm tb_copied lam_exp".split())
        mix_mm, mix_b, mix_u, sgu_hi, sgu_lo = map(sem, "mix_mm mix_b mix_u sgu_hi sgu_lo".split())
        pair_free, pair_ready, l_half, l_done, near_done, far_done, max_done, exp_done = map(sem, "pair_free pair_ready l_half l_done near_done far_done max_done exp_done".split())
        comb_done, t_done, t_copied, o_mm, o_done, step = map(sem, "comb_done t_done t_copied o_mm o_done step".split())
        sq_sum, o_root, o_inv, o_ready, ot_mm, o_hi, o_lo = map(sem, "sq_sum o_root o_inv o_ready ot_mm o_hi o_lo".split())
        PAIR = 2 * TT
        rising = list(range(1, TT, 2))
        ORDER = [(a, i) for i in rising + [i - 1 for i in rising[::-1]] for a in range(2)]
        FAR = [0]
        for m in range(PAIR):
            FAR.append(FAR[-1] + (ORDER[m][1] >= 2))
        block = ctx.enter_context(nc.Block())

        @block.sync
        def _(sp):
            sp.dma_start(rb[:], rel_bias).then_inc(small_ld, 16)
            sp.dma_start(hot[:], bucket_hot).then_inc(small_ld, 16)
            sp.dma_start(lam[:].rearrange("p a b -> p (a b)"), lam_p.to_broadcast([P, 4 * DH])).then_inc(small_ld, 16)
            sp.dma_start(sg[:], subln_col).then_inc(small_ld, 16)
            sp.dma_start(wt, sgu_wt).then_inc(w_ld, 16)
            for half in range(2):
                src = sgu_b.rearrange("(a b) t -> b a t", b=2)[half:half + 1].to_broadcast([DH, SGU_G // 2, P])
                sp.dma_start(bt[half * DH:half * DH + DH], src).then_inc(bt_ld, 16)
            sp.wait_ge(tb_copied, HEADS_A)
            rows = logit_row[:, 0:HEADS_A * HALF].rearrange("p (h m) -> p h m", h=HEADS_A)
            sp.dma_start(tbl_d.rearrange("h p m -> p h m"), rows[:, :, 0:RLEN]).then_inc(tb_st, 16)
            sp.wait_ge(tb_st, 16)
            skew = bass.AP(tensor=tbl_d.tensor, offset=P - 1, ap=[[RLEN - 1, P], [P * RLEN, HEADS_A], [1, 2 * P]])
            sp.dma_start(tb[:], skew).then_inc(tb_ld, 16)
            sp.wait_ge(o_mm, HEADS_A * TT)
            for k in range(2):
                sp.dma_start(stage[:, (2 + k) * D:(3 + k) * D], w_out[:, k]).then_inc(wo_ld[k], 16)

        @block.gpsimd
        def _(pool):
            pool.wait_ge(w_ld, 16)
            nc.gpsimd.affine_select(out=wt, in_=wt, compare_op=ALU.is_ge, fill=0.0, base=0,
                                    pattern=[[0, SGU_G], [1, P]], channel_multiplier=-1).then_inc(masked, 1)

            pool.wait_ge(tb_ld, 16)
            nc.gpsimd.affine_select(out=tb[:], in_=tb[:], compare_op=ALU.is_ge, fill=LOWEST, base=P,
                                    pattern=[[0, HEADS_A], [-1, 2 * P]], channel_multiplier=1).then_inc(tb_masked, 1)

        @block.scalar
        def _(act):
            for h in range(HEADS_A):
                act.wait_ge(tb_mm, HEADS_A)
                nc.scalar.activation(logit_row[:, h * HALF:h * HALF + RLEN], ps_row[:, h * HALF:h * HALF + RLEN],
                                     ACT.Copy).then_inc(tb_copied, 1)
            act.wait_ge(ready, 2)
            nc.scalar.activation(lame[:], lamd[:], ACT.Exp).then_inc(lam_exp, 1)
            for c in range(TT):
                act.wait_ge(mix_u, c + 1)
                nc.scalar.activation(cat_hi[:, 0:4, c * P:c * P + P], att[:, c % 2, 0:SW].rearrange("p (g t) -> p g t", g=4),
                                     ACT.Copy).then_inc(sgu_hi, 1)

            def far_part(w, m):
                i = ORDER[m][1]
                if i < 2:
                    return
                n = (i - 1) * P
                act.wait_ge(l_done, PAIR * w + m + 1)
                if m >= NL:
                    act.wait_ge(comb_done, PAIR * w + m - NL + 1)
                nc.scalar.activation(logit[:, m % NL, :, 0:n], ps_far[:, :, 0:n], ACT.Identity,
                                     bias=far_pair[:, ORDER[m][0]:ORDER[m][0] + 1]).then_inc(far_done, 1)

            def exps(w, m):
                n = (ORDER[m][1] + 1) * P
                act.wait_ge(max_done, PAIR * w + m + 1)
                for c in range(2):
                    nc.scalar.activation(logit[:, m % NL, c, 0:n], logit[:, m % NL, c, 0:n], ACT.Exp, bias=nmax[:, m % 2, c:c + 1],
                                         accum_out=ssum[:, m % 2, c:c + 1]).then_inc(exp_done, 1)

            def copy_t(w, m):
                n = ORDER[m][1] + 1
                act.wait_ge(t_done, PAIR * w + m + 1)
                if m >= 2:
                    act.wait_ge(o_mm, PAIR * w + m - 1)
                nc.scalar.activation(att_t[:, m % 2, 0:n], ps_t[:, 0:n], ACT.Copy).then_inc(t_copied, 1)

            def squares(w, m):
                i = ORDER[m][1]
                act.wait_ge(o_done, PAIR * w + m + 1)
                if m:
                    act.wait_ge(sq_sum, PAIR * w + m)
                col = 2 * w + ORDER[m][0]
                nc.scalar.activation(sq_row[:], o_all[:, i, bass.ds(col * VD, VD)], ACT.Square,
                                     accum_out=osq[:, i, bass.ds(col, 1)]).then_inc(sq_sum, 1)

            with loop(nc, act, 0, HEADS_A // 2) as w:
                act.wait_ge(pair_free, w + 1)
                nc.scalar.activation(pair_qk[:, 2:4], z_t[:, bass.ds(8 + 2 * w, 2)], ACT.Copy).then_inc(pair_ready, 1)
                far_part(w, 0)
                far_part(w, 1)
                exps(w, 0)
                for m in range(PAIR):
                    if m + 1 < PAIR:
                        exps(w, m + 1)
                    if m + 2 < PAIR:
                        far_part(w, m + 2)
                    copy_t(w, m)
                    if m >= 1:
                        squares(w, m - 1)
                squares(w, PAIR - 1)
                act.wait_ge(sq_sum, PAIR * w + PAIR)
            nc.scalar.activation(ort[:], osq[:], ACT.Sqrt, bias=eps[:], scale=1.0 / VD).then_inc(o_root, 1)
            for t in range(TT):
                act.wait_ge(ot_mm, t + 1)
                nc.scalar.activation(cat_hi[:, 4:8, t * P:t * P + P], ps_l[:, t % 2, 0:SW].rearrange("p (g t) -> p g t", g=4),
                                     ACT.Copy, scale=sgs[:]).then_inc(o_hi, 1)

        @block.tensor
        def _(pe):
            pe.wait_ge(ready, 4)
            for h in range(HEADS_A):
                mm = pe.matmul(ps_row[:, h * HALF:h * HALF + RLEN], rbb[:, h], hot[:], start=True, stop=True)
            mm.then_inc(tb_mm, HEADS_A)
            pe.wait_ge(tb_copied, HEADS_A)
            pe.wait_ge(masked, 1)
            for c in range(TT):
                if c >= 2:
                    pe.wait_ge(mix_b, c - 1)
                for g in range(SGU_G):
                    r = g % 2 * DH
                    mm = pe.matmul(ps_l[r:r + DH, c % 2, g // 2 * P:g // 2 * P + P], z_n[:, c, g * DH:g * DH + DH], wt[:, g],
                                   start=True, stop=True)
                mm.then_inc(mix_mm, 1)

            def logits(w, m):
                g = PAIR * w + m
                hh, i = ORDER[m]
                if m == 0:
                    pe.wait_ge(pair_ready, 3 * w + 3)
                if m:
                    pe.wait_ge(near_done, g)
                if FAR[m]:
                    pe.wait_ge(far_done, FAR[PAIR] * w + FAR[m])
                split = max(i - 1, 0) * P
                for c in range(2):
                    cuts = [0, HALF if c == 0 else HALF // 2, split]
                    parts = [(ps_far[:, c, k0:min(k1, split)], k0, min(k1, split)) for k0, k1 in zip(cuts, cuts[1:]) if k0 < split]
                    parts.append((ps_near[:, c, 0:(i + 1) * P - split], split, (i + 1) * P))
                    for dst, k0, k1 in parts:
                        mm = pe.matmul(dst, pair_qk[c * DH:c * DH + DH, hh, i * P:i * P + P],
                                       pair_qk[c * DH:c * DH + DH, 2 + hh, k0:k1], start=True, stop=True)
                    if c == 0:
                        mm.then_inc(l_half, 1)
                        pe.wait_ge(l_half, g + 1)
                mm.then_inc(l_done, 1)

            def turn(w, m):
                pe.wait_ge(comb_done, PAIR * w + m + 1)
                if m:
                    pe.wait_ge(t_copied, PAIR * w + m)
                for j in range(ORDER[m][1] + 1):
                    mm = pe.transpose(ps_t[:, j], att[:, m % 2, j * P:j * P + P], ident[:])
                mm.then_inc(t_done, 1)

            def values(w, m):
                i = ORDER[m][1]
                pe.wait_ge(t_copied, PAIR * w + m + 1)
                if m >= 2:
                    pe.wait_ge(o_done, PAIR * w + m - 1)
                col = SW + (2 * w + ORDER[m][0]) * VD
                for j in range(i + 1):
                    mm = pe.matmul(ps_o[:, m % 2, 0:VD], att_t[:, m % 2, j], z_n[:, j, bass.ds(col, VD)],
                                   start=(j == 0), stop=(j == i))
                mm.then_inc(o_mm, 1)

            pe.wait_ge(mix_b, TT)
            with loop(nc, pe, 0, HEADS_A // 2) as w:
                pe.wait_ge(pair_free, w + 1)
                logits(w, 0)
                logits(w, 1)
                for m in range(PAIR):
                    if m + 2 < PAIR:
                        logits(w, m + 2)
                    if m >= 1:
                        values(w, m - 1)
                    turn(w, m)
                values(w, PAIR - 1)
            for t in range(TT):
                if t >= 2:
                    pe.wait_ge(o_lo, t - 1)
                pe.wait_ge(o_ready, t + 1)
                for h in range(HEADS_A):
                    mm = pe.transpose(ps_l[:, t % 2, h * P:h * P + P], o_all[:, t, h * VD:h * VD + VD], ident[:])
                mm.then_inc(ot_mm, 1)

        @block.vector
        def _(dve):
            ch = Chain(dve, step)
            nc.vector.memset(eps[:], EPS).then_inc(ready, 1)
            dve.wait_ge(small_ld, 64)
            nc.vector.tensor_copy(rbb[:], rb[:].unsqueeze(2).to_broadcast([RB, HEADS_A, P])).then_inc(ready, 1)
            ch.done(nc.vector.tensor_tensor(lamw[:], lam[:, 0:4:2], lam[:, 1:4:2], ALU.mult))
            ch.sync()
            nc.vector.tensor_reduce(lamd[:], lamw[:], AX.X, ALU.add).then_inc(ready, 1)
            nc.vector.tensor_scalar(sgs[:], sg[:], 1.0 - LAM_INIT, None, ALU.mult).then_inc(ready, 1)
            dve.wait_ge(lam_exp, 1)
            ch.done(nc.vector.scalar_tensor_tensor(out=neglam[:], in0=lame[:, 1:2], scalar=-LAM_INIT, in1=lame[:, 0:1],
                                                   op0=ALU.add, op1=ALU.subtract))
            dve.wait_ge(tb_copied, HEADS_A)
            ch.done(nc.vector.tensor_copy(far[:], logit_row[:, 0:HEADS_A * HALF:HALF]))
            dve.wait_ge(bt_ld, 32)

            def mixed(c):
                a = att[:, c % 2, 0:SW].rearrange("p (g t) -> p g t", g=4)
                dve.wait_ge(mix_mm, c + 1)
                if c >= 2:
                    dve.wait_ge(sgu_lo, c - 1)
                nc.vector.tensor_tensor(a, ps_l[:, c % 2, 0:SW].rearrange("p (g t) -> p g t", g=4), bt[:], ALU.add).then_inc(mix_b, 1)
                dve.wait_ge(mix_b, c + 1)
                nc.vector.tensor_tensor(a, a, z_t[:, 0:4, c * P:c * P + P], ALU.mult).then_inc(mix_u, 1)

            def mixed_lo(c):
                a = att[:, c % 2, 0:SW].rearrange("p (g t) -> p g t", g=4)
                dve.wait_ge(sgu_hi, c + 1)
                nc.vector.tensor_tensor(cat_lo[:, 0:4, c * P:c * P + P], a, cat_hi[:, 0:4, c * P:c * P + P].bitcast(F32),
                                        ALU.subtract).then_inc(sgu_lo, 1)

            mixed(0)
            for c in range(1, TT):
                mixed(c)
                mixed_lo(c - 1)
            mixed_lo(TT - 1)
            dve.wait_ge(sgu_lo, TT)
            dve.wait_ge(tb_masked, 1)
            dve.wait_ge(tb_st, 16)
            ch.sync()

            def near(w, m):
                i = ORDER[m][1]
                k0, width = (i - 1) * P if i else 0, 2 * P if i else P
                dve.wait_ge(l_done, PAIR * w + m + 1)
                if m >= NL:
                    dve.wait_ge(comb_done, PAIR * w + m - NL + 1)
                bias = tb[:, bass.ds(2 * w + ORDER[m][0], 1), 2 * P - width:2 * P].to_broadcast([P, 2, width])
                nc.vector.tensor_tensor(logit[:, m % NL, :, k0:k0 + width], ps_near[:, :, 0:width], bias, ALU.add).then_inc(near_done, 1)

            def maximum(w, m):
                g = PAIR * w + m
                n = (ORDER[m][1] + 1) * P
                dve.wait_ge(near_done, g + 1)
                if FAR[m + 1]:
                    dve.wait_ge(far_done, FAR[PAIR] * w + FAR[m + 1])
                ch.done(nc.vector.tensor_reduce(mx[:, m % 2], logit[:, m % NL, :, 0:n], AX.X, ALU.max))
                ch.sync()
                nc.vector.tensor_scalar(nmax[:, m % 2], mx[:, m % 2], -1.0, None, ALU.mult).then_inc(max_done, 1)

            def combine(w, m):
                g = PAIR * w + m
                n = (ORDER[m][1] + 1) * P
                b = m % 2
                dve.wait_ge(exp_done, 2 * g + 2)
                if m >= 2:
                    dve.wait_ge(o_done, PAIR * w + m - 1)
                ch.done(nc.vector.reciprocal(sinv[:, b], ssum[:, b]))
                ch.sync()
                ch.done(nc.vector.scalar_tensor_tensor(out=fac[:, b:b + 1], in0=ssum[:, b, 0:1], scalar=neglam[:], in1=sinv[:, b, 1:2],
                                                       op0=ALU.mult, op1=ALU.mult))
                ch.sync()
                if m >= 2:
                    dve.wait_ge(t_done, PAIR * w + m - 1)
                nc.vector.scalar_tensor_tensor(out=att[:, b, 0:n], in0=logit[:, m % NL, 1, 0:n], scalar=fac[:, b:b + 1],
                                               in1=logit[:, m % NL, 0, 0:n], op0=ALU.mult, op1=ALU.add).then_inc(comb_done, 1)

            def output(w, m):
                dve.wait_ge(o_mm, PAIR * w + m + 1)
                col = (2 * w + ORDER[m][0]) * VD
                nc.vector.tensor_scalar(o_all[:, ORDER[m][1], bass.ds(col, VD)], ps_o[:, m % 2, 0:VD], sinv[:, m % 2, 0:1], None,
                                        ALU.mult).then_inc(o_done, 1)

            ch.reset()
            dve.sem_inc(pair_free, 1)
            with loop(nc, dve, 0, HEADS_A // 2) as w:
                nc.vector.tensor_scalar(pair_qk[:, 0:2], z_t[:, bass.ds(4 + 2 * w, 2)], DH ** -0.5, None, ALU.mult).then_inc(pair_ready, 1)
                nc.vector.tensor_copy(far_pair[:], far[:, bass.ds(2 * w, 2)]).then_inc(pair_ready, 1)
                for m in range(2):
                    near(w, m)
                    maximum(w, m)
                for m in range(PAIR):
                    combine(w, m)
                    if m + 2 < PAIR:
                        near(w, m + 2)
                        maximum(w, m + 2)
                    if m >= 1:
                        output(w, m - 1)
                output(w, PAIR - 1)
                dve.wait_ge(o_done, PAIR * w + PAIR)
                dve.sem_inc(pair_free, 1)
                ch.reset()
            dve.wait_ge(o_root, 1)
            nc.vector.reciprocal(oin[:], ort[:]).then_inc(o_inv, 1)
            dve.wait_ge(o_inv, 1)

            def normed(t):
                o = o_all[:, t].rearrange("p (h n) -> p h n", h=HEADS_A)
                nc.vector.tensor_tensor(o, o, oin[:, t].unsqueeze(2).to_broadcast([P, HEADS_A, VD]), ALU.mult).then_inc(o_ready, 1)

            normed(0)
            normed(1)
            for t in range(TT):
                if t + 2 < TT:
                    normed(t + 2)
                dve.wait_ge(o_hi, t + 1)
                nc.vector.scalar_tensor_tensor(out=cat_lo[:, 4:8, t * P:t * P + P],
                                               in0=ps_l[:, t % 2, 0:SW].rearrange("p (g t) -> p g t", g=4), scalar=sgs[:],
                                               in1=cat_hi[:, 4:8, t * P:t * P + P].bitcast(F32),
                                               op0=ALU.mult, op1=ALU.subtract).then_inc(o_lo, 1)


def out_project_and_norm(nc, x, w_out, h_hi, h_lo, mod_cols, gain1, ident, stage, wo_ld, cols, columns, x_mid):
    with ExitStack() as ctx:
        sb = lambda n, s, d=F32: ctx.enter_context(nc.sbuf_tensor(n, s, d))
        sem = lambda n: ctx.enter_context(nc.semaphore("op_" + n))
        hf = stage[:, 0:2 * D].rearrange("p (b k t) -> p b k t", b=2, k=DC)
        raw = stage[:, 2 * D:4 * D].rearrange("p (b n) -> p b n", b=2)
        w_hi = sb("wo_hi", [P, DC, D], F32R)
        w_lo = sb("wo_lo", [P, DC, D], F32R)
        xt = sb("x_in_rows", [P, 2, D])
        xm = sb("x_mid_rows", [P, 2, D])
        xr = sb("x_mid_scaled", [P, 2, D])
        sq_out = sb("squares_y", [P, 2, HALF])
        sq_out2 = sb("squares_x", [P, D])
        ssy, rty, iny = sb("ssy", [P, TT]), sb("rty", [P, TT]), sb("iny", [P, TT])
        ssx, rtx, inx = sb("ssx", [P, TT]), sb("rtx", [P, TT]), sb("inx", [P, TT])
        eps = sb("eps_f5", [P, 1])
        ps_y = columns.ps
        ps_x = ctx.enter_context(nc.psum_tensor("ps_xo", [P, 2, DC, P], F32))
        x_ld = [sem("x_ld0"), sem("x_ld1")]
        x_st = [sem("x_st0"), sem("x_st1")]
        w_hid, w_lod, y_mm, ysq, yrt, yin, y_gain, x_new = map(sem, "w_hi w_lo y_mm ysq yrt yin y_gain x_new".split())
        xsq, xrt, xin, xr_done, xt_done, hf_done, hi_done, lo_done, ready = map(sem, "xsq xrt xin xr xt hf hi lo ready".split())
        block = ctx.enter_context(nc.Block())

        @block.sync
        def _(sp):
            for k in range(2, DC):
                sp.wait_ge(w_lod, k - 1)
                sp.dma_start(raw[:, k % 2], w_out[:, k]).then_inc(wo_ld[k % 2], 16)
            for t in range(TT):
                if t >= 2:
                    sp.wait_ge(x_new, t - 1)
                sp.dma_start(xt[:, t % 2], x[t * P:t * P + P]).then_inc(x_ld[t % 2], 16)
                if t == 1:
                    for n in range(2):
                        sp.wait_ge(w_lod, DC - 1 + n)
                        sp.dma_start(columns.raw[:, n], cols[n]).then_inc(columns.loaded[n], 16)
                if t >= 1:
                    sp.wait_ge(x_new, t)
                    sp.dma_start(x_mid[t * P - P:t * P], xm[:, (t - 1) % 2]).then_inc(x_st[(t - 1) % 2], 16)
            sp.wait_ge(x_new, TT)
            sp.dma_start(x_mid[S - P:S], xm[:, 1]).then_inc(x_st[1], 16)
            for b in range(2):
                sp.wait_ge(x_st[b], 16 * TT // 2)

        @block.scalar
        def _(act):
            for k in range(DC):
                act.wait_ge(wo_ld[k % 2], 16 * (k // 2 + 1))
                nc.scalar.activation(w_hi[:, k], raw[:, k % 2], ACT.Copy).then_inc(w_hid, 1)
            act.wait_ge(ready, 1)

            def y_root(t):
                act.wait_ge(y_mm, t + 1)
                if t >= 1:
                    act.wait_ge(ysq, t)
                nc.scalar.activation(sq_out[:], ps_y[:, t % 2], ACT.Square, accum_out=ssy[:, t:t + 1]).then_inc(ysq, 1)
                act.wait_ge(ysq, t + 1)
                nc.scalar.activation(rty[:, t:t + 1], ssy[:, t:t + 1], ACT.Sqrt, bias=eps[:], scale=1.0 / D).then_inc(yrt, 1)

            def x_root(t):
                act.wait_ge(x_new, t + 1)
                if t >= 1:
                    act.wait_ge(xsq, t)
                nc.scalar.activation(sq_out2[:], xm[:, t % 2], ACT.Square, accum_out=ssx[:, t:t + 1]).then_inc(xsq, 1)
                act.wait_ge(xsq, t + 1)
                nc.scalar.activation(rtx[:, t:t + 1], ssx[:, t:t + 1], ACT.Sqrt, bias=eps[:], scale=1.0 / D).then_inc(xrt, 1)

            def hi(t):
                act.wait_ge(hf_done, 2 * t + 2)
                nc.scalar.activation(h_hi[:, :, t * P:t * P + P], hf[:, t % 2], ACT.Copy).then_inc(hi_done, 1)

            for t in range(TT):
                y_root(t)
                x_root(t)
                if t >= 1:
                    hi(t - 1)
                if t == 3:
                    for n in range(2):
                        act.wait_ge(columns.loaded[n], 16)
                        nc.scalar.activation(columns.hi[:, n], columns.raw[:, n], ACT.Copy).then_inc(columns.hi_done, 1)
            hi(TT - 1)

        @block.tensor
        def _(pe):
            def chunk(t, k):
                for i, (c, w) in enumerate(((h_hi, w_hi), (h_hi, w_lo), (h_lo, w_hi))):
                    for half in range(2):
                        mm = pe.matmul(ps_y[:, t % 2, half], c[:, k, t * P:t * P + P], w[:, k, half * HALF:half * HALF + HALF],
                                       start=(k == 0 and i == 0), stop=(k == DC - 1 and i == 2))
                if k == DC - 1:
                    mm.then_inc(y_mm, 1)

            def project(t):
                pe.wait_ge(y_gain, t - 1)
                for k in range(DC):
                    chunk(t, k)

            def turn(t):
                pe.wait_ge(xr_done, t + 1)
                if t >= 2:
                    pe.wait_ge(hf_done, 2 * (t - 2) + 1)
                for k in range(DC):
                    mm = pe.transpose(ps_x[:, t % 2, k], xr[:, t % 2, k * P:k * P + P], ident[:])
                mm.then_inc(xt_done, 1)

            for k in range(DC):
                pe.wait_ge(w_lod, k + 1)
                chunk(0, k)
                chunk(1, k)
            for t in range(2, TT):
                project(t)
                turn(t - 2)

            def first_half(n):
                pe.wait_ge(columns.lo_done, n + 1)
                pe.wait_ge(lo_done, TT // 2)
                pe.wait_ge(y_gain, TT - 1 + n)
                for k in range(DC):
                    for i, (w, h) in enumerate(((columns.hi, h_hi), (columns.hi, h_lo), (columns.lo, h_hi))):
                        pe.matmul(columns.ps[:, n, 0], w[:, n, k], h[:, k, 0:HALF], start=(k == 0 and i == 0), stop=(k == DC - 1 and i == 2))

            first_half(0)
            turn(TT - 2)
            first_half(1)
            turn(TT - 1)

        @block.vector
        def _(dve):
            nc.vector.memset(eps[:], EPS).then_inc(ready, 1)
            for k in range(DC):
                dve.wait_ge(w_hid, k + 1)
                nc.vector.tensor_tensor(w_lo[:, k], raw[:, k % 2], w_hi[:, k].bitcast(F32), ALU.subtract).then_inc(w_lod, 1)

            def residual(t):
                b = t % 2
                dve.wait_ge(yrt, t + 1)
                nc.vector.reciprocal(iny[:, t:t + 1], rty[:, t:t + 1]).then_inc(yin, 1)
                dve.wait_ge(yin, t + 1)
                if t >= 2:
                    dve.wait_ge(x_st[b], 16 * (t // 2))
                    dve.wait_ge(xr_done, t - 1)
                    dve.wait_ge(xsq, t - 1)
                nc.vector.scalar_tensor_tensor(out=xm[:, b], in0=ps_y[:, b].rearrange("p a b -> p (a b)"), scalar=iny[:, t:t + 1],
                                               in1=gain1[:], op0=ALU.mult, op1=ALU.mult).then_inc(y_gain, 1)
                dve.wait_ge(y_gain, t + 1)
                dve.wait_ge(x_ld[b], 16 * (t // 2 + 1))
                nc.vector.tensor_tensor(xm[:, b], xm[:, b], xt[:, b], ALU.add).then_inc(x_new, 1)

            def scaled(t):
                b = t % 2
                dve.wait_ge(xrt, t + 1)
                nc.vector.reciprocal(inx[:, t:t + 1], rtx[:, t:t + 1]).then_inc(xin, 1)
                dve.wait_ge(xin, t + 1)
                if t >= 2:
                    dve.wait_ge(xt_done, t - 1)
                nc.vector.tensor_scalar(xr[:, b], xm[:, b], inx[:, t:t + 1], None, ALU.mult).then_inc(xr_done, 1)

            def modulated(t):
                dve.wait_ge(xt_done, t + 1)
                if t >= 2:
                    dve.wait_ge(lo_done, t - 1)
                    dve.wait_ge(hi_done, t - 1)
                affine_cols(nc, dve, hf[:, t % 2], ps_x[:, t % 2], mod_cols[:, 2], mod_cols[:, 3], hf_done, 2 * t)
                dve.wait_ge(hi_done, t + 1)
                nc.vector.tensor_tensor(h_lo[:, :, t * P:t * P + P], hf[:, t % 2], h_hi[:, :, t * P:t * P + P].bitcast(F32),
                                        ALU.subtract).then_inc(lo_done, 1)

            for t in range(TT):
                residual(t)
                scaled(t)
                if t >= 1:
                    modulated(t - 1)
                if t == 3:
                    for n in range(2):
                        dve.wait_ge(columns.hi_done, n + 1)
                        nc.vector.tensor_tensor(columns.lo[:, n], columns.raw[:, n], columns.hi[:, n].bitcast(F32),
                                                ALU.subtract).then_inc(columns.lo_done, 1)
            modulated(TT - 1)


def layout(d):
    L = {}
    L["x"] = d["x"][0]
    L["c_col"] = d["c"].reshape(DC, P).T
    rows = [0, 1, 2, 5, 3, 4]
    L["w_ada"] = d["w_ada"][0].reshape(DC, P, NADA, D).transpose(2, 0, 1, 3)[rows]
    L["b_ada"] = d["b_ada"].reshape(1, NADA, D)[:, rows].reshape(1, NADA * D)
    L["norm_g"] = d["norm_g"][0]
    L["g_col"] = d["norm_g"][0].reshape(4, DC, P).transpose(2, 0, 1)
    w = d["w_in"][0].reshape(DC, P, 10, COLW).transpose(2, 1, 0, 3)
    L["w_in"] = w[[0, 1, 4, 5, 6, 7, 2, 3, 8, 9]]
    L["sgu_wt"] = d["sgu_w"][0].transpose(2, 0, 1)
    L["sgu_b"] = d["sgu_b"][0]
    L["sgu_ln"] = np.concatenate([d["sgu_ln_g"], d["sgu_ln_b"]])
    L["lam_p"] = d["diff_lambda"].reshape(1, 4 * DH)
    L["subln_col"] = d["diff_subln_g"].reshape(VD, 1)
    L["rel_bias"] = d["rel_bias"]
    n = np.maximum(255 - np.arange(RLEN), 0)
    exact = RB // 2
    big = exact + (np.log(np.maximum(n, 1).astype(np.float32) / exact) / math.log(128 / exact) * (RB - exact)).astype(np.int32)
    bucket = np.where(n < exact, n, np.minimum(big, RB - 1))
    L["bucket_hot"] = (np.arange(RB)[:, None] == bucket[None]).astype(np.float32)
    L["w_out"] = d["w_out"][0].reshape(DC, P, D).transpose(1, 0, 2)
    cols = np.empty((NQ + ETILES, P, DC, P), d["peer_u"].dtype)
    cols[:NQ] = d["peer_w_query"][0].reshape(DC, P, NQ, P).transpose(2, 1, 0, 3)
    cols[NQ:] = d["peer_u"][0].reshape(P, ETILES, DC, P).transpose(1, 3, 2, 0)
    L["cols"] = cols
    L["keys_t"] = d["peer_sub_keys"][0].transpose(3, 0, 1, 2).reshape(P, HC, NKEY)
    L["v_cols"] = d["peer_v"][0].reshape(P, ETILES, D).transpose(1, 0, 2)
    return {k: np.ascontiguousarray(v) for k, v in L.items()}


def build(nc, t, scratch="Internal"):
    dram = lambda n, s: nc.dram_tensor(n, s, F32, kind=scratch).ap()
    x_mid = dram("x_mid", (S, D))
    tbl = dram("distance_rows", (HEADS_A, P, RLEN))
    scores = dram("scores", (TT, HEADS, P, 2, NKEY))
    act_d = dram("expert_act", (ETILES, P, S))
    gate_d = dram("expert_gate", (S // GBLK, P, ETILES, GBLK))
    with ExitStack() as ctx:
        sb = lambda n, s, d=F32: ctx.enter_context(nc.sbuf_tensor(n, s, d))
        v_in = [ctx.enter_context(nc.semaphore(n)) for n in ("v_in0", "v_in1")]
        a_in = [ctx.enter_context(nc.semaphore(n)) for n in ("a_in0", "a_in1")]
        gain2 = sb("gain2", [P, D])
        stage = sb("stage", [P, 4 * D])
        with ExitStack() as inner:
            sb = lambda n, s, d=F32: inner.enter_context(nc.sbuf_tensor(n, s, d))
            h_hi = sb("h_hi", [P, DC, S], F32R)
            h_lo = sb("h_lo", [P, DC, S], F32R)
            ident = sb("ident_f", [P, P])
            mod_cols = sb("mod_cols", [P, 4, DC])
            gain1 = sb("gain1", [P, D])
            wo_ld = [inner.enter_context(nc.semaphore(n)) for n in ("w_out_in0", "w_out_in1")]
            with nc.sbuf_tensor("z_t", [P, 12, S], F32) as z_t, nc.sbuf_tensor("z_n", [P, TT, 2 * SW], F32) as z_n:
                with ExitStack() as first:
                    ones, c_silu = (first.enter_context(nc.sbuf_tensor(n, s, F32)) for n, s in (("ones_f", [P, P]), ("c_silu", [P, DC])))
                    w = Weights(nc, first, t["w_in"], stage)
                    x_t = z_t[:, 4:4 + DC]
                    spent = modulate_and_norm(nc, t["x"], t["c_col"], t["w_ada"], t["b_ada"], t["g_col"], ident, ones, c_silu, x_t,
                                              mod_cols, gain1, gain2, w, z_t, z_n)
                    in_project(nc, w, t["w_ada"], t["b_ada"], t["norm_g"], t["g_col"], ident, ones, c_silu, x_t, mod_cols,
                               gain1, gain2, h_hi, h_lo, z_t, z_n, t["sgu_ln"], spent)
                mix(nc, z_t, z_n, stage, t["sgu_wt"], t["sgu_b"], t["lam_p"], t["subln_col"], t["rel_bias"],
                    t["bucket_hot"], tbl, ident, h_hi, h_lo, t["w_out"], wo_ld)
            columns = Columns(nc, inner, stage)
            out_project_and_norm(nc, t["x"], t["w_out"], h_hi, h_lo, mod_cols, gain1, ident, stage, wo_ld, t["cols"], columns, x_mid)
            route_and_up(nc, h_hi, h_lo, stage, columns, ident, t["cols"], t["keys_t"], t["v_cols"], v_in, a_in, scores, act_d, gate_d)
        down_and_finish(nc, stage, act_d, gate_d, t["v_cols"], v_in, a_in, x_mid, gain2, t["out"])


def kernel(**inputs):
    import concourse.bacc as bacc
    from concourse.bass_utils import run_bass_kernel_spmd

    arrays = layout({k: np.asarray(v) for k, v in inputs.items()})
    nc = bacc.Bacc("TRN2", target_bir_lowering=False, num_devices=1)
    t = {k: nc.dram_tensor(k, v.shape, mybir.dt.from_np(v.dtype), kind="ExternalInput").ap() for k, v in arrays.items()}
    t["out"] = nc.dram_tensor("out", (S, D), F32, kind="ExternalOutput").ap()
    build(nc, t)
    r = run_bass_kernel_spmd(nc, [arrays], core_ids=[0])
    return r.results[0]["out"].reshape(1, S, D)
```
